# Optimizing a Trainium2 kernel written in Bass

```python
import math
import jax, jax.numpy as jnp
from jax import lax
import numpy as np

D_MODEL = 1024
BATCH = 1
SEQ = 128
DEPTH = 1
DEC_BATCH = 1
DEC_SEQ = 512
PAST_LEN = 128

GRID_W = 64
EPS = 1e-6
D_A = D_MODEL // 4
NH_A = 4
HD_A = D_A // NH_A
CHUNK = 128
D_B = D_MODEL // 2
HD_B = 64
NH_B = D_B // HD_B
NA_WIN_R = 8
NA_WIN_C = 16
ATTN_SCALE = HD_B ** -0.5
D_C = D_MODEL - D_A - D_B
SSM_CH = 16
SSM_G = D_C // SSM_CH
SSM_P = 64
DT_MIN = 0.001
DT_MAX = 0.1
D_IN = 2 * D_A + 3 * D_B + D_C
IN_SPLITS = (2 * D_A, 2 * D_A + D_B, 2 * D_A + 2 * D_B, 2 * D_A + 3 * D_B)
N_EXPERTS = 64
TOP_K = 8
N_EXP_GROUPS = 8
TOPK_GROUPS = 4
D_EXPERT = 256
D_SHARED = 256
ROUTE_SCALE = 2.5
MOE_BLOCK = 128

kernel_name = 'hybrid_prefix_diffusion_step'

def _rmsnorm(x, g):
    x32 = x.astype(jnp.float32)
    y = x32 * lax.rsqrt(jnp.mean(x32 * x32, axis=-1, keepdims=True) + EPS)
    return (y * g.astype(jnp.float32)).astype(x.dtype)

def _chunk_mlp(pa, sgu_g, w_sp, b_sp):
    b_, l_, _ = pa.shape
    z = jax.nn.gelu(pa)
    u, v = z[..., :D_A], z[..., D_A:]
    v32 = v.astype(jnp.float32)
    mu = jnp.mean(v32, axis=-1, keepdims=True)
    var = jnp.mean(jnp.square(v32 - mu), axis=-1, keepdims=True)
    v = ((v32 - mu) * lax.rsqrt(var + EPS) * sgu_g.astype(jnp.float32)).astype(pa.dtype)
    v = v.reshape(b_, l_ // CHUNK, CHUNK, NH_A, HD_A)
    s = jnp.einsum('hij,bnjhd->bnihd', w_sp, v) + b_sp.T[:, :, None]
    return u * s.reshape(b_, l_, D_A)

def _ctx_attn(q, k, v):
    b_, l_ = q.shape[:2]
    qb = q.reshape(b_, l_ // CHUNK, CHUNK, NH_B, HD_B).transpose(1, 0, 2, 3, 4)

    def block(qi):
        s = jnp.einsum('bqhd,bkhd->bhqk', qi, k).astype(jnp.float32) * ATTN_SCALE
        pr = jax.nn.softmax(s, axis=-1).astype(v.dtype)
        return jnp.einsum('bhqk,bkhd->bqhd', pr, v)

    o = lax.map(block, qb)
    return o.transpose(1, 0, 2, 3, 4).reshape(b_, l_, D_B)

def _nat_attn(q, k, v, ck, cv, rpb):
    b_, l_ = q.shape[:2]
    rows = l_ // GRID_W
    wr = min(NA_WIN_R, rows)
    qg = q.reshape(b_, rows, GRID_W, NH_B, HD_B)
    kg = k.reshape(b_, rows, GRID_W, NH_B, HD_B)
    vg = v.reshape(b_, rows, GRID_W, NH_B, HD_B)
    cols = jnp.arange(GRID_W)
    col_start = jnp.clip(cols - NA_WIN_C // 2, 0, GRID_W - NA_WIN_C)
    col_idx = col_start[:, None] + jnp.arange(NA_WIN_C)[None, :]
    col_off = col_idx - cols[:, None] + (NA_WIN_C - 1)
    n_win = wr * NA_WIN_C

    def row_fn(r):
        rs = jnp.clip(r - wr // 2, 0, rows - wr)
        q_r = lax.dynamic_index_in_dim(qg, r, axis=1, keepdims=False)
        k_win = lax.dynamic_slice_in_dim(kg, rs, wr, axis=1)[:, :, col_idx]
        v_win = lax.dynamic_slice_in_dim(vg, rs, wr, axis=1)[:, :, col_idx]
        row_off = rs + jnp.arange(wr) - r + (NA_WIN_R - 1)
        bias = rpb[:, row_off][:, :, col_off].transpose(0, 2, 1, 3)
        s_win = (jnp.einsum('bchd,bwcjhd->bhcwj', q_r, k_win).astype(jnp.float32) * ATTN_SCALE
                 + bias.astype(jnp.float32)[None])
        s_ctx = jnp.einsum('bchd,blhd->bhcl', q_r, ck).astype(jnp.float32) * ATTN_SCALE
        s = jnp.concatenate([s_win.reshape(b_, NH_B, GRID_W, n_win), s_ctx], axis=-1)
        pr = jax.nn.softmax(s, axis=-1).astype(v.dtype)
        p_win = pr[..., :n_win].reshape(b_, NH_B, GRID_W, wr, NA_WIN_C)
        p_ctx = pr[..., n_win:]
        return (jnp.einsum('bhcwj,bwcjhd->bchd', p_win, v_win)
                + jnp.einsum('bhcl,blhd->bchd', p_ctx, cv))

    o = lax.map(row_fn, jnp.arange(rows))
    return o.transpose(1, 0, 2, 3, 4).reshape(b_, l_, D_B)

def _lin_combine(e1, e2):
    a1, b1 = e1
    a2, b2 = e2
    return a1 * a2, a2 * b1 + b2

def _diag_scan(a, bu, h0):
    bu = bu.at[:, 0].add(a * h0)
    a_full = jnp.broadcast_to(a, bu.shape)
    _, h = lax.associative_scan(_lin_combine, (a_full, bu), axis=1)
    return h

def _s5(pc, p, h0):
    b_, l_, _ = pc.shape
    f32 = jnp.float32
    u = pc.astype(f32).reshape(b_, l_, SSM_G, SSM_CH)
    lam = lax.complex(p['ssm_a_re'].astype(f32), p['ssm_a_im'].astype(f32))
    dt = jnp.exp(p['ssm_log_dt'].astype(f32))[..., None]
    lam_bar = jnp.exp(lam * dt)
    b_bar = ((lam_bar - 1) / lam)[..., None] * lax.complex(
        p['ssm_b_re'].astype(f32), p['ssm_b_im'].astype(f32))
    c_mat = lax.complex(p['ssm_c_re'].astype(f32), p['ssm_c_im'].astype(f32))
    if h0 is None:
        h0 = jnp.zeros((b_, 2, SSM_G, SSM_P), jnp.complex64)
    uc = u.astype(jnp.complex64)
    h_f = _diag_scan(lam_bar[0], jnp.einsum('blgc,gpc->blgp', uc, b_bar[0]), h0[:, 0])
    h_b = jnp.flip(_diag_scan(lam_bar[1], jnp.flip(jnp.einsum('blgc,gpc->blgp', uc, b_bar[1]), axis=1),
                              h0[:, 1]), axis=1)
    y = (jnp.real(jnp.einsum('blgp,gcp->blgc', h_f, c_mat[0]))
         + jnp.real(jnp.einsum('blgp,gcp->blgc', h_b, c_mat[1]))
         + p['ssm_d'].astype(f32).reshape(SSM_G, SSM_CH) * u)
    y = jax.nn.gelu(y.reshape(b_, l_, D_C)).astype(pc.dtype)
    out = y * jax.nn.sigmoid(y @ p['w_glu'] + p['b_glu'])
    h_last = jnp.stack([h_f[:, -1], h_b[:, 0]], axis=1)
    return out, h_last

def _moe(h, p):
    b_, l_, d_ = h.shape
    f32 = jnp.float32
    xf = h.reshape(-1, d_)
    t_ = xf.shape[0]
    scores = jax.nn.sigmoid(xf.astype(f32) @ p['w_router'].astype(f32))
    sel = scores + p['b_router'].astype(f32)
    grp = lax.top_k(sel.reshape(t_, N_EXP_GROUPS, N_EXPERTS // N_EXP_GROUPS), 2)[0].sum(-1)
    gidx = lax.top_k(grp, TOPK_GROUPS)[1]
    gmask = jax.nn.one_hot(gidx, N_EXP_GROUPS, dtype=f32).sum(1) > 0
    emask = jnp.repeat(gmask, N_EXPERTS // N_EXP_GROUPS, axis=1)
    _, idx = lax.top_k(jnp.where(emask, sel, -jnp.inf), TOP_K)
    wts = jnp.take_along_axis(scores, idx, axis=1)
    wts = wts / jnp.sum(wts, axis=-1, keepdims=True) * ROUTE_SCALE
    e_flat = idx.reshape(-1)
    tok_flat = jnp.repeat(jnp.arange(t_, dtype=jnp.int32), TOP_K)
    g_flat = wts.reshape(-1)
    order = jnp.argsort(e_flat)
    e_s, tok_s, g_s = e_flat[order], tok_flat[order], g_flat[order]
    counts = jnp.bincount(e_flat, length=N_EXPERTS)
    starts = jnp.cumsum(counts) - counts
    pcounts = (counts + MOE_BLOCK - 1) // MOE_BLOCK * MOE_BLOCK
    pends = jnp.cumsum(pcounts)
    pstarts = pends - pcounts
    dest = pstarts[e_s] + (jnp.arange(t_ * TOP_K) - starts[e_s])
    n_blocks = (t_ * TOP_K + N_EXPERTS * (MOE_BLOCK - 1)) // MOE_BLOCK + 1
    n_pad = n_blocks * MOE_BLOCK
    row_tok = jnp.full((n_pad,), t_, jnp.int32).at[dest].set(tok_s)
    row_gate = jnp.zeros((n_pad,), f32).at[dest].set(g_s)
    blk_exp = jnp.minimum(jnp.searchsorted(pends, jnp.arange(n_blocks) * MOE_BLOCK, side='right'),
                          N_EXPERTS - 1)
    x_pad = jnp.concatenate([xf, jnp.zeros((1, d_), xf.dtype)], axis=0)

    def step(acc, blk):
        toks, gates, e = blk
        xb = x_pad[toks]
        hb = jax.nn.silu(xb @ p['w_e_gate'][e]) * (xb @ p['w_e_up'][e])
        yb = (hb @ p['w_e_down'][e]) * gates[:, None].astype(xb.dtype)
        return acc.at[toks].add(yb), None

    acc, _ = lax.scan(step, jnp.zeros((t_ + 1, d_), xf.dtype),
                      (row_tok.reshape(n_blocks, MOE_BLOCK), row_gate.reshape(n_blocks, MOE_BLOCK), blk_exp))
    shared = (jax.nn.silu(xf @ p['w_s_gate']) * (xf @ p['w_s_up'])) @ p['w_s_down']
    return (acc[:t_] + shared).reshape(b_, l_, d_)

def _layer(x, mod, p, ctx):
    sh1, sc1, g1, sh2, sc2, g2 = jnp.split(mod, 6, axis=-1)
    b_, l_, _ = x.shape
    h = _rmsnorm(x, p['g_pre_mix']) * (1 + sc1) + sh1
    pa, pq, pk, pv, pc = jnp.split(h @ p['w_in'], IN_SPLITS, axis=-1)
    q = pq.reshape(b_, l_, NH_B, HD_B)
    k = pk.reshape(b_, l_, NH_B, HD_B)
    v = pv.reshape(b_, l_, NH_B, HD_B)
    ya = _chunk_mlp(pa, p['sgu_g'], p['w_sp'], p['b_sp'])
    if ctx is None:
        yb = _ctx_attn(q, k, v)
        yc, h_last = _s5(pc, p, None)
        state = (k, v, jnp.real(h_last), jnp.imag(h_last))
    else:
        ck, cv, s_re, s_im = ctx
        yb = _nat_attn(q, k, v, ck, cv, p['rpb'])
        yc, _ = _s5(pc, p, lax.complex(s_re.astype(jnp.float32), s_im.astype(jnp.float32)))
        state = None
    mixed = jnp.concatenate([ya, yb, yc], axis=-1) @ p['w_out']
    x = x + g1 * _rmsnorm(mixed, p['g_post_mix'])
    h = _rmsnorm(x, p['g_pre_ffn']) * (1 + sc2) + sh2
    x = x + g2 * _rmsnorm(_moe(h, p), p['g_post_ffn'])
    return x, state

def setup_inputs(seed: int = 0) -> dict:
    key = jax.random.key(seed)
    ks = iter(jax.random.split(key, 48))
    f32 = jnp.float32

    def nrm(shape, scale):
        return jax.random.normal(next(ks), shape, f32) * scale

    L = DEPTH
    return {
        'x_prompt': nrm((BATCH, SEQ, D_MODEL), 1.0),
        'x_sample': nrm((DEC_BATCH, DEC_SEQ, D_MODEL), 1.0),
        'cache_k': nrm((DEC_BATCH, DEPTH, PAST_LEN, NH_B, HD_B), 1.0),
        'cache_v': nrm((DEC_BATCH, DEPTH, PAST_LEN, NH_B, HD_B), 1.0),
        'state_ssm_re': nrm((DEC_BATCH, DEPTH, 2, SSM_G, SSM_P), 0.1),
        'state_ssm_im': nrm((DEC_BATCH, DEPTH, 2, SSM_G, SSM_P), 0.1),
        'c': nrm((DEC_BATCH, D_MODEL), 1.0),
        'c_ctx': nrm((D_MODEL,), 1.0),
        'g_pre_mix': 1.0 + nrm((L, D_MODEL), 0.02),
        'g_post_mix': 1.0 + nrm((L, D_MODEL), 0.02),
        'g_pre_ffn': 1.0 + nrm((L, D_MODEL), 0.02),
        'g_post_ffn': 1.0 + nrm((L, D_MODEL), 0.02),
        'w_ada': nrm((L, D_MODEL, 6 * D_MODEL), 0.5 * D_MODEL ** -0.5),
        'b_ada': nrm((L, 6 * D_MODEL), 0.02),
        'w_in': nrm((L, D_MODEL, D_IN), D_MODEL ** -0.5),
        'w_out': nrm((L, D_A + D_B + D_C, D_MODEL), (D_A + D_B + D_C) ** -0.5),
        'sgu_g': 1.0 + nrm((L, D_A), 0.02),
        'w_sp': nrm((L, NH_A, CHUNK, CHUNK), CHUNK ** -0.5),
        'b_sp': 1.0 + nrm((L, NH_A, CHUNK), 0.02),
        'rpb': nrm((L, NH_B, 2 * NA_WIN_R - 1, 2 * NA_WIN_C - 1), 0.1),
        'ssm_a_re': -0.5 + nrm((L, 2, SSM_G, SSM_P), 0.01),
        'ssm_a_im': math.pi * jnp.arange(SSM_P, dtype=f32) + nrm((L, 2, SSM_G, SSM_P), 0.01),
        'ssm_log_dt': jax.random.uniform(next(ks), (L, 2, SSM_G), f32, math.log(DT_MIN), math.log(DT_MAX)),
        'ssm_b_re': nrm((L, 2, SSM_G, SSM_P, SSM_CH), (2 * SSM_CH) ** -0.5),
        'ssm_b_im': nrm((L, 2, SSM_G, SSM_P, SSM_CH), (2 * SSM_CH) ** -0.5),
        'ssm_c_re': nrm((L, 2, SSM_G, SSM_CH, SSM_P), SSM_P ** -0.5),
        'ssm_c_im': nrm((L, 2, SSM_G, SSM_CH, SSM_P), SSM_P ** -0.5),
        'ssm_d': nrm((L, D_C), 1.0),
        'w_glu': nrm((L, D_C, D_C), D_C ** -0.5),
        'b_glu': nrm((L, D_C), 0.02),
        'w_router': nrm((L, D_MODEL, N_EXPERTS), D_MODEL ** -0.5),
        'b_router': nrm((L, N_EXPERTS), 0.01),
        'w_e_gate': nrm((L, N_EXPERTS, D_MODEL, D_EXPERT), D_MODEL ** -0.5),
        'w_e_up': nrm((L, N_EXPERTS, D_MODEL, D_EXPERT), D_MODEL ** -0.5),
        'w_e_down': nrm((L, N_EXPERTS, D_EXPERT, D_MODEL), D_EXPERT ** -0.5),
        'w_s_gate': nrm((L, D_MODEL, D_SHARED), D_MODEL ** -0.5),
        'w_s_up': nrm((L, D_MODEL, D_SHARED), D_MODEL ** -0.5),
        'w_s_down': nrm((L, D_SHARED, D_MODEL), D_SHARED ** -0.5),
    }

def reference(x_prompt, x_sample, cache_k, cache_v, state_ssm_re, state_ssm_im, c, c_ctx,
              g_pre_mix, g_post_mix, g_pre_ffn, g_post_ffn, w_ada, b_ada, w_in, w_out,
              sgu_g, w_sp, b_sp, rpb, ssm_a_re, ssm_a_im, ssm_log_dt, ssm_b_re, ssm_b_im,
              ssm_c_re, ssm_c_im, ssm_d, w_glu, b_glu, w_router, b_router,
              w_e_gate, w_e_up, w_e_down, w_s_gate, w_s_up, w_s_down):
    xp = x_prompt
    xs = x_sample
    new_k, new_v, new_re, new_im = [], [], [], []
    for l in range(DEPTH):
        p = {
            'g_pre_mix': g_pre_mix[l], 'g_post_mix': g_post_mix[l],
            'g_pre_ffn': g_pre_ffn[l], 'g_post_ffn': g_post_ffn[l],
            'w_in': w_in[l], 'w_out': w_out[l],
            'sgu_g': sgu_g[l], 'w_sp': w_sp[l], 'b_sp': b_sp[l], 'rpb': rpb[l],
            'ssm_a_re': ssm_a_re[l], 'ssm_a_im': ssm_a_im[l], 'ssm_log_dt': ssm_log_dt[l],
            'ssm_b_re': ssm_b_re[l], 'ssm_b_im': ssm_b_im[l],
            'ssm_c_re': ssm_c_re[l], 'ssm_c_im': ssm_c_im[l], 'ssm_d': ssm_d[l],
            'w_glu': w_glu[l], 'b_glu': b_glu[l],
            'w_router': w_router[l], 'b_router': b_router[l],
            'w_e_gate': w_e_gate[l], 'w_e_up': w_e_up[l], 'w_e_down': w_e_down[l],
            'w_s_gate': w_s_gate[l], 'w_s_up': w_s_up[l], 'w_s_down': w_s_down[l],
        }
        mod_ctx = (jax.nn.silu(c_ctx) @ w_ada[l] + b_ada[l])[None, None, :]
        mod_lat = (jax.nn.silu(c) @ w_ada[l] + b_ada[l])[:, None, :]
        xp, (k_l, v_l, s_re_l, s_im_l) = _layer(xp, mod_ctx, p, None)
        xs, _ = _layer(xs, mod_lat, p, (cache_k[:, l], cache_v[:, l], state_ssm_re[:, l], state_ssm_im[:, l]))
        new_k.append(k_l)
        new_v.append(v_l)
        new_re.append(s_re_l)
        new_im.append(s_im_l)
    return (xp, xs, jnp.stack(new_k, axis=1), jnp.stack(new_v, axis=1),
            jnp.stack(new_re, axis=1), jnp.stack(new_im, axis=1))


_drawn_inputs = setup_inputs


def setup_inputs(seed=0):
    import zlib

    import numpy as np

    out = dict(_drawn_inputs(seed))
    spreads = {}
    factors = {'state_ssm_re': 3.247,
     'state_ssm_im': 3.384,
     'g_pre_mix': 3.064,
     'g_post_mix': 3.498,
     'g_post_ffn': 26.595,
     'sgu_g': 3.042,
     'b_sp': 4.659,
     'rpb': 5.41,
     'ssm_a_re': 21.441,
     'b_glu': 5.482,
     'cache_k': 8.0,
     'cache_v': 8.0}
    for name, (base, spread) in spreads.items():
        noise = np.random.default_rng([zlib.crc32(name.encode()), seed]).standard_normal(out[name].shape)
        drawn = base * np.exp(spread * noise) if base else spread * noise
        out[name] = __import__('jax').numpy.asarray(drawn.astype(out[name].dtype))
    for name, factor in factors.items():
        out[name] = (out[name] * factor).astype(out[name].dtype)
    return out
```

```python
from contextlib import ExitStack

import numpy as np
import concourse.bass as bass
from concourse import mybir

F32 = mybir.dt.float32
BF16 = mybir.dt.bfloat16
I32 = mybir.dt.int32
ALU = mybir.AluOpType
ACT = mybir.ActivationFunctionType
AX = mybir.AxisListType

P = 128
D = 1024
KD = D // P
LAT, CTX = 512, 128
TOK = LAT + CTX
NT = TOK // P
CTX_T = NT - 1
D_A, D_B, D_C = 256, 512, 256
D_IN = 2 * D_A + 3 * D_B + D_C
NH_A = 4
NH, HD = 8, 64
GW, GR = 64, 8
WIN = 16
QC = P // GR
KC = 32
KC0 = [0, 8, 24, 32]
KEYS = GR * KC
KIND = [0, 1, 1, 2]
SHIFT = 16
BW = SHIFT + KC
G, NS, CH = 16, 64, 16
GD = 2 * G
Q = 8
CL, CC = LAT // Q, CTX // Q
NC = CL + CC
SL = CL + 1 + CC + 1
NR = SL - 1
NE, TOPK, NG, TOPG = 64, 8, 8, 4
F = 256
EPS = 1e-6
ROUTE_SCALE = 2.5
BLK = TOK // P
U = 4
MAXOV = 40
NBLK = NE + MAXOV
NEG = -1e30
TAKEN = -2e30
MASKED = -30000.0
TWO_PI = 2 * np.pi
PI_HI = 6.28125
PI_MID = 0.00193500518798828125
PI_LO = float(TWO_PI - PI_HI - PI_MID)
ROUND = 1.5 * 2.0 ** 23


class Shared:
    pass


class Chain:

    def __init__(self, sem):
        self.sem, self.n = sem, 0

    def on(self, eng):
        self.eng = eng
        return self

    def __call__(self, ins):
        self.n += 1
        ins.then_inc(self.sem, 1)
        self.eng.wait_ge(self.sem, self.n)


def project(nc, k, a):
    bank, ring, hT, ident = k.bank, k.ring, k.hT, k.ident
    scope = ExitStack()
    sem = k.scoped_sem(scope)
    sb = k.scoped(scope)
    N1 = 3

    xb = [sb(f"x_tile{i}", [P, D]) for i in range(2)]
    shift_b, scale_b = sb("shift_b", [P, D]), sb("scale_b", [P, D])
    cT = sb("cT", [P, 2, KD])
    cS = sb("cS", [P, KD, 33])
    b12 = sb("b12", [12, 512])
    sel = sb("sel", [12, 12, 33])
    modrow = sb("modrow", [33, 2, D])
    grow = sb("grow", [33, D])
    ss = sb("ss", [P, NT, 2])
    ssum = sb("ssum", [P, NT])
    rms = sb("rms", [P, NT])
    rstd = sb("rstd", [P, NT])
    vt = [sb(f"v_tile{i}", [P, D_B]) for i in range(2)]
    kctx = sb("kctx", [P, D_B])
    rpbT = sb("rpbT", [NH * 15, BW + QC])
    rpb_in, skew_out = k.soft["rpb_in"], k.soft["skew_out"]
    aa = sb("aa", [GD, 2, P])
    h0s = sb("h0s", [GD, P])
    ldt = sb("ldt", [P, GD])
    BA, BB = sb("BA", [P, GD, CH]), sb("BB", [P, GD, CH])
    C1, C2 = sb("C1", [P, GD, CH]), sb("C2", [P, GD, CH])
    Dg = sb("Dg", [CH, G, CH])
    dB = sb("dB", [CH, D_C])
    pr, pim = sb("pr", [P, Q + 1, GD]), sb("pim", [P, Q + 1, GD])
    xpr, xpi = sb("xpr", [P, Q, GD]), sb("xpi", [P, Q, GD])
    wpr, wpi = sb("wpr", [P, Q, GD]), sb("wpi", [P, Q, GD])
    sm = [sb(f"sm{i}", [P, GD]) for i in range(14)]
    A, B = k.ring[3], k.mixed_flat[:, 0:GD * P]
    cc = [A[:, i * 512:(i + 1) * 512].rearrange("p (q n) -> p q n", q=4) for i in range(2)]
    B1, B2 = (A[:, i * 512:(i + 1) * 512].rearrange("p (g c) -> p g c", c=CH) for i in (2, 3))
    cm = [k.mixed_flat[:, GD * P + i * P:GD * P + (i + 1) * P] for i in range(4)]
    kF, kB = (k.mixed_flat[:, i * 256:(i + 1) * 256].rearrange("p (g c) -> p g c", c=CH) for i in (18, 19))

    c_in, small_in, x_in = sem("c_in"), sem("small_in"), [k.soft[f"x_in{t}"] for t in range(NT)]
    w1_in = [sem(f"w1_in{i}") for i in range(N1)]
    cs_zero, cs_ready = sem("cs_zero"), sem("cs_ready")
    acc_ready, acc_taken = sem("acc_ready"), sem("acc_taken")
    grow_in = k.soft["grow_in"]
    row_ready, mod_stored, mod_b = sem("row_ready"), [k.soft[f"mod_stored{g}"] for g in range(6)], k.soft["mod_b"]
    sq_done, ssum_done, rms_done = sem("sq_done"), sem("ssum_done"), sem("rms_done")
    h_ready = sem("h_ready")
    v_sent, kctx_sent = [sem(f"v_sent{i}") for i in range(2)], sem("kctx_sent")
    s5_in, s5_t, dt_raw, trig_arg, trig = sem("s5_in"), sem("s5_t"), sem("dt_raw"), sem("trig_arg"), sem("trig")
    mag_arg, mag = sem("mag_arg"), sem("mag")
    s5_small_taken, c_t = sem("s5_small_taken"), sem("c_t")
    X_ready, XT_t, XT_taken, K_ready, K_taken = sem("X_ready"), sem("XT_t"), sem("XT_taken"), sem("K_ready"), sem("K_taken")
    mats, mat_out, lag_out, rot_ready, rot_out = sem("mats"), sem("mat_out"), sem("lag_out"), sem("rot_ready"), sem("rot_out")
    NS5 = 18
    w_ada = a["w_ada"][0].rearrange("(p k) n -> p k n", k=KD)
    w_in = a["w_in"][0].rearrange("(p k) n -> p k n", k=KD)
    loads = [("ada", c) for c in range(8)] + [("in", c) for c in range(4)] + [("ada", c) for c in range(8, 12)] + [("in", 4)]
    def halves(*tiles):
        return [("xT", (t, h)) for t in tiles for h in range(2)]
    jobs = [("ada", c) for c in range(7)] + halves(0, 1) + [("ada", 7)] + halves(2, 3)
    jobs += [("pa", t) for t in range(4)] + halves(4) + [("pa", 4)]
    for what in "qk":
        jobs += [(what, (j, part)) for j in range(4) for part in range(2)]
    jobs += [("kctx", 0)] + [("v", t) for t in range(NT)] + [("ada", c) for c in range(8, 12)]
    jobs += [("pc", s) for s in range(4)]
    at = {job: n for n, job in enumerate(jobs)}
    NB = 3
    last_of = {("in", 0): ("pa", NT - 1), ("in", 1): ("q", (3, 1)), ("in", 2): ("k", (3, 1)),
               ("in", 3): ("v", NT - 1), ("in", 4): ("pc", 3)}
    last_job = [at[last_of.get(ld, ld)] for ld in loads]

    def w1(n):
        return ring[n % N1][:, :].rearrange("p (k n) -> p k n", k=KD)

    x_src = [a["x_sample"][0][t * P:(t + 1) * P, :] for t in range(4)] + [a["x_prompt"][0]]
    gained = [1, 2, 4, 5]
    group_gain = {1: a["g_pre_mix"], 2: a["g_post_mix"], 4: a["g_pre_ffn"], 5: a["g_post_ffn"]}

    block = scope.enter_context(nc.Block())

    @block.sync
    def _(sp):
        for v, c in enumerate((a["c_ctx"].rearrange("(p k) -> p k", k=KD), a["c"][0].rearrange("(p k) -> p k", k=KD))):
            sp.dma_start(cT[:, v, :], c).then_inc(c_in, 16)
        def load(n):
            kind, c = loads[n]
            if n >= N1:
                sp.wait_ge(acc_ready, last_job[n - N1] + 1)
            w = 512 if kind == "ada" else min(512, D_IN - 512 * c)
            src = (w_ada if kind == "ada" else w_in)[:, :, 512 * c:512 * c + w]
            sp.dma_start(w1(n)[:, :, 0:w], src).then_inc(w1_in[n % N1], 16)
        n_first = loads.index(("in", 3)) + 1
        for n in range(n_first):
            load(n)
            if n == 0:
                sp.dma_start(b12[:, :], a["b_ada"][0].rearrange("(c n) -> c n", c=12)).then_inc(small_in, 16)
            if n == 2:
                for t in range(2):
                    sp.dma_start(xb[t][:, :], x_src[t]).then_inc(x_in[t], 16)
        for m in range(3):
            if m == 0:
                sp.wait_ge(XT_taken, GD // 4)
            else:
                sp.wait_ge(mats, m)
            src = (B if m == 0 else A[:, :])
            sp.dma_start(k.matD[m], src).then_inc(mat_out, 16)
        load(n_first)
        sp.wait_ge(K_taken, 1)
        for s in range(Q):
            sp.dma_start(k.lagD[:, :, Q - 1 - s, :], kB[s * CH:(s + 1) * CH, :, :]).then_inc(lag_out, 16)
        for s in range(Q - 1):
            sp.dma_start(k.lagD[:, :, 2 * Q - 2 - s, :], kF[s * CH:(s + 1) * CH, :, :]).then_inc(lag_out, 16)
        load(n_first + 1)
        sp.wait_ge(rot_ready, 1)
        sp.dma_start(k.rotD[0], A[:, 0:GD * SL]).then_inc(rot_out, 16)
        sp.dma_start(k.rotD[1], B[:, 0:GD * SL]).then_inc(rot_out, 16)
        for n in range(n_first + 2, len(loads)):
            load(n)
        sp.wait_ge(lag_out, 16 * (2 * Q - 1))
        sp.wait_ge(rot_out, 32)
        sp.wait_ge(mat_out, 48)

    @block.gpsimd
    def _(pool):
        pl = k.pool_chain.on(pool)
        pl(pool.memset(ident[:, :], 0.0))
        pl(pool.affine_select(out=ident[:, :], in_=ident[:, :], compare_op=ALU.not_equal, fill=1.0,
                              base=0, pattern=[[-1, P]], channel_multiplier=1))
        pl(pool.memset(sel[:, :, :], 0.0))
        pl(pool.affine_select(out=sel[:, :, 0:33:32], in_=sel[:, :, 0:33:32], compare_op=ALU.not_equal, fill=1.0,
                              base=0, pattern=[[1, 12], [0, 2]], channel_multiplier=-1))
        pool.memset(cS[:, :, :], 0.0).then_inc(cs_zero, 1)
        pl(pool.memset(k.flip[:, :], 0.0))
        for total in (CL - 1, 2 * (CL + 1) + CC - 1):
            w = k.flip[0:NR, 0:NR]
            pl(pool.affine_select(out=w, in_=w, compare_op=ALU.not_equal, fill=1.0,
                                  base=-total, pattern=[[1, NR]], channel_multiplier=1))
        pl(pool.memset(k.flip80[:, :], 0.0))
        for total in (CL - 1, CL + NC - 1):
            w = k.flip80[0:NC, 0:NC]
            pl(pool.affine_select(out=w, in_=w, compare_op=ALU.not_equal, fill=1.0,
                                  base=-total, pattern=[[1, NC]], channel_multiplier=1))
        pool.memset(k.eps[:, :], EPS).then_inc(k.consts, 1)

        def gain(g):
            for r in (0, 32):
                pool.dma_start(grow[r:r + 1, :], group_gain[g][0:1, :]).then_inc(grow_in, 16)

        def store(g):
            if g in gained:
                pool.wait_ge(row_ready, gained.index(g) + 1)
            else:
                pool.wait_ge(acc_taken, at[("ada", 2 * g + 1)] + 1)
            for v, r in enumerate((0, 32)):
                pool.dma_start(k.modD[v:v + 1, g, :], modrow[r:r + 1, g % 2, :]).then_inc(mod_stored[g], 16)

        def spread(v):
            pool.dma_start(shift_b[:, :], k.modD[v, 0].partition_broadcast(P)).then_inc(mod_b, 16)
            pool.dma_start(scale_b[:, :], k.modD[v, 1].partition_broadcast(P)).then_inc(mod_b, 16)
        gain(1)
        store(0)
        store(1)
        pool.wait_ge(mod_stored[0], 32)
        pool.wait_ge(mod_stored[1], 32)
        spread(1)
        gain(2)
        for t in range(2, NT):
            pool.wait_ge(acc_ready, at[("xT", (t - 2, 1))] + 1)
            pool.dma_start(xb[t % 2][:, :], x_src[t]).then_inc(x_in[t], 16)
        pool.wait_ge(h_ready, 4)
        spread(0)
        store(2)
        store(3)
        gain(4)
        pl(pool.memset(rpbT[:, :], 0.0))
        pool.dma_start(rpbT[:, SHIFT + QC - 16:SHIFT + QC + 15], a["rpb"][0].rearrange("h r c -> (h r) c")).then_inc(rpb_in, 16)
        pool.wait_ge(rpb_in, 16)
        for c in range(QC):
            pool.dma_start(k.skewD[c].rearrange("h r c -> (h r) c"),
                           rpbT[:, QC - 1 - c:QC - 1 - c + BW]).then_inc(skew_out, 16)
        store(4)
        gain(5)
        store(5)
        for g in range(2, 6):
            pool.wait_ge(mod_stored[g], 32)
        pool.wait_ge(skew_out, 16 * QC)

    @block.scalar
    def _(act):
        at_ = k.act_chain.on(act)
        act.wait_ge(c_in, 32)
        act.wait_ge(cs_zero, 1)
        for v, r in enumerate((0, 32)):
            act.activation(cS[:, :, r], cT[:, v, :], ACT.Silu).then_inc(cs_ready, 1)
        n_in = 0

        def load(dst, src):
            nonlocal n_in
            n_in += 1
            act.dma_start(dst, src).then_inc(s5_in, 16)
        for i, prm in enumerate((a["ssm_a_re"], a["ssm_a_im"])):
            for h in range(2):
                load(aa[:, i, h * NS:(h + 1) * NS], prm[0].rearrange("d g p -> (d g) p"))
        load(h0s[:, 0:NS], a["state_ssm_re"][0, 0].rearrange("d g p -> (d g) p"))
        load(h0s[:, NS:P], a["state_ssm_im"][0, 0].rearrange("d g p -> (d g) p"))
        load(ldt[:, :], a["ssm_log_dt"][0].rearrange("d g -> (d g)").partition_broadcast(P))
        bre, bim = (x[0].rearrange("d g p c -> p (d g) c") for x in (a["ssm_b_re"], a["ssm_b_im"]))
        load(B1[0:NS], bre)
        load(B1[NS:P], bim)
        load(B2[0:NS], bim)
        load(B2[NS:P], bre)
        for i, (top, low) in enumerate(((a["ssm_c_re"], a["ssm_c_im"]), (a["ssm_c_im"], a["ssm_c_re"]))):
            for h, prm in enumerate((top, low)):
                load(cc[i][:, :, h * NS:(h + 1) * NS], prm[0].rearrange("d (e g) c p -> (g c) (d e) p", e=2))
        load(dB[:, :], a["ssm_d"][0].partition_broadcast(CH))
        act.dma_start(k.sgu_b[:, :], a["sgu_g"][0].partition_broadcast(P)).then_inc(s5_in, 16)
        act.dma_start(k.wsp[:, :, :], a["w_sp"][0].rearrange("h i j -> i h j")).then_inc(s5_in, 16)
        n_in += 2
        assert n_in == NS5
        act.wait_ge(k.consts, 1)

        def square(t):
            act.wait_ge(x_in[t], 16)
            for h in range(2):
                if t or h:
                    act.wait_ge(sq_done, 2 * t + h)
                act.activation(bank[7][:, :], xb[t % 2][:, h * 512:(h + 1) * 512], ACT.Square,
                               accum_out=ss[:, t, h:h + 1]).then_inc(sq_done, 1)

        def root(t):
            act.wait_ge(ssum_done, t + 1)
            act.activation(rms[:, t:t + 1], ssum[:, t:t + 1], ACT.Sqrt, bias=k.eps[:, :],
                           scale=1.0 / D).then_inc(rms_done, 1)

        def s5_functions():
            act.wait_ge(s5_in, 16 * NS5)
            act.activation(sm[0][:, :], ldt[:, :], ACT.Exp).then_inc(dt_raw, 1)
            act.wait_ge(mag_arg, 1)
            act.activation(sm[3][:, :], sm[1][:, :], ACT.Exp).then_inc(mag, 1)
            act.activation(sm[4][:, :], sm[1][:, :], ACT.Exp, scale=float(Q)).then_inc(mag, 1)
            act.wait_ge(trig_arg, 1)
            act.activation(sm[5][:, :], sm[2][:, :], ACT.Sin).then_inc(trig, 1)
            act.activation(sm[6][:, :], sm[2][:, :], ACT.Sin, scale=0.5).then_inc(trig, 1)

        square(0)
        square(1)
        root(0)
        root(1)
        for n, (kind, i) in enumerate(jobs):
            src = bank[n % NB]
            if (kind, i) == ("pa", 2):
                s5_functions()
            act.wait_ge(acc_ready, n + 1)
            if kind == "ada":
                g, h = i // 2, i % 2
                if g >= 2:
                    act.wait_ge(mod_stored[g - 2], 32)
                act.activation(modrow[:, g % 2, h * 512:(h + 1) * 512], src[0:33, :], ACT.Copy).then_inc(acc_taken, 1)
            elif kind == "xT":
                t, h = i
                act.activation(hT[:, 4 * h:4 * h + 4, t * P:(t + 1) * P],
                               src[:, :].rearrange("p (k n) -> p k n", k=4), ACT.Copy).then_inc(acc_taken, 1)
                if h == 1 and t + 2 < NT:
                    square(t + 2)
                    root(t + 2)
            elif kind == "pa":
                act.activation(k.z[:, i, :], src[:, :], ACT.Gelu_apprx_tanh).then_inc(acc_taken, 1)
            elif kind in "qk":
                j, part = i
                dst = k.qT if kind == "q" else k.kT
                tok = slice(0, LAT) if part == 0 else slice(LAT, TOK)
                dst, src = dst[:, j, tok], src[:, 0:(LAT, CTX)[part]]
                if kind == "q" and part == 0:
                    dst = dst.rearrange("p (t r c) -> p r t c", t=4, c=QC)
                    src = src.rearrange("p (r t c) -> p r t c", t=4, c=QC)
                act.activation(dst, src, ACT.Copy, scale=HD ** -0.5 if kind == "q" else 1.0).then_inc(acc_taken, 1)
            elif kind == "kctx":
                act.activation(kctx[:, :], src[:, :], ACT.Copy).then_inc(acc_taken, 1)
                act.wait_ge(acc_taken, n + 1)
                act.dma_start(k.outs["new_k"][0, 0].rearrange("s h d -> s (h d)"), kctx[:, :]).then_inc(kctx_sent, 16)
            elif kind == "v":
                if i >= 2:
                    act.wait_ge(v_sent[i % 2], 16 * (i // 2))
                dst = vt[i % 2] if i < CTX_T else k.vctx
                act.activation(dst[:, :], src[:, :], ACT.Copy).then_inc(acc_taken, 1)
                act.wait_ge(acc_taken, n + 1)
                to = k.vD[i * P:(i + 1) * P, :] if i < CTX_T else k.outs["new_v"][0, 0].rearrange("s h d -> s (h d)")
                act.dma_start(to, dst[:, :]).then_inc(v_sent[i % 2], 16)
            elif kind == "pc":
                act.activation(k.pc[0:NC, :, 2 * i:2 * i + 2, :].rearrange("p g s c -> p s g c"),
                               src[0:NC, :].rearrange("p (s g c) -> p s g c", s=2, c=CH), ACT.Copy).then_inc(acc_taken, 1)
        act.wait_ge(kctx_sent, 16)
        act.wait_ge(v_sent[0], 48)
        act.wait_ge(v_sent[1], 32)

    @block.vector
    def _(dve):
        v = k.dve_chain.on(dve)
        tt, ts, stt, cp = dve.tensor_tensor, dve.tensor_scalar, dve.scalar_tensor_tensor, dve.tensor_copy

        def total(t):
            dve.wait_ge(sq_done, 2 * t + 2)
            tt(ssum[:, t:t + 1], ss[:, t, 0:1], ss[:, t, 1:2], ALU.add).then_inc(ssum_done, 1)
        total(0)
        total(1)
        def rows(g):
            dve.wait_ge(acc_taken, at[("ada", 2 * g + 1)] + 1)
            dve.wait_ge(grow_in, 32 * (gained.index(g) + 1))
            for r in (0, 32):
                row = modrow[r:r + 1, g % 2, :]
                if g in (1, 4):
                    last = stt(row, row, 1.0, grow[r:r + 1, :], ALU.add, ALU.mult)
                else:
                    last = tt(row, row, grow[r:r + 1, :], ALU.mult)
            last.then_inc(row_ready, 1)
        rows(1)
        for t in range(NT):
            if t >= 2:
                total(t)
            dve.wait_ge(mod_b, 32 if t < CTX_T else 64)
            dve.wait_ge(rms_done, t + 1)
            x = xb[t % 2][:, :]
            v(dve.reciprocal(rstd[:, t:t + 1], rms[:, t:t + 1]))
            v(stt(x, x, rstd[:, t:t + 1], scale_b[:, :], ALU.mult, ALU.mult))
            tt(x, x, shift_b[:, :], ALU.add).then_inc(h_ready, 1)
        rows(2)
        dt, er, ph, mag1, mag8, sn, sh, ar, ai = sm[0], sm[1], sm[2], sm[3], sm[4], sm[5], sm[6], sm[7], sm[8]
        dve.wait_ge(s5_t, 1)
        v(cp(ar[:, :], bank[5][:, 0:GD]))
        v(cp(ai[:, :], bank[5][:, GD:2 * GD]))
        v(cp(k.h0[:, :], bank[5][:, 2 * GD:3 * GD]))
        v(ts(B2[0:NS], B2[0:NS], -1.0, None, ALU.mult))
        dve.wait_ge(dt_raw, 1)
        tt(er[:, :], ar[:, :], dt[:, :], ALU.mult).then_inc(mag_arg, 1)
        v(tt(ph[:, :], ai[:, :], dt[:, :], ALU.mult))
        turns = sm[9]
        v(ts(turns[:, :], ph[:, :], 1.0 / TWO_PI, None, ALU.mult))
        v(ts(turns[:, :], turns[:, :], ROUND, None, ALU.add))
        v(ts(turns[:, :], turns[:, :], -ROUND, None, ALU.add))
        for part in (PI_HI, PI_MID, PI_LO):
            v(stt(ph[:, :], turns[:, :], -part, ph[:, :], ALU.mult, ALU.add))
        ts(ph[:, :], ph[:, :], 3.1415925, -3.1415925, ALU.min, ALU.max).then_inc(trig_arg, 1)
        dve.wait_ge(c_t, 1)
        for i, dst in enumerate((C1, C2)):
            src = bank[6 - i][:, 0:4 * P] if i == 0 else bank[4][:, 0:4 * P]
            src = src.rearrange("p (g c) -> p g c", c=CH)
            ts(dst[0:NS], src[0:NS], 1.0 if i == 0 else -1.0, None, ALU.mult)
            v(ts(dst[NS:P], src[NS:P], -1.0, None, ALU.mult))
        dve.wait_ge(trig, 2)
        dve.wait_ge(mag, 2)
        wr, wi = sm[10], sm[11]
        v(tt(sm[9][:, :], sh[:, :], sh[:, :], ALU.mult))
        v(ts(wr[:, :], sm[9][:, :], -2.0, 1.0, ALU.mult, ALU.add))
        v(cp(wi[:, :], sn[:, :]))

        def cmul(orr, oi, xr, xi, yr, yi, width, view=lambda z: z):
            t = [view(z[:, 0:width]) for z in cm]
            tt(t[0], xr, yr, ALU.mult)
            tt(t[1], xi, yi, ALU.mult)
            tt(t[2], xr, yi, ALU.mult)
            v(tt(t[3], xi, yr, ALU.mult))
            tt(orr, t[0], t[1], ALU.subtract)
            v(tt(oi, t[2], t[3], ALU.add))

        dve.memset(pr[:, 0, :], 1.0)
        dve.memset(pim[:, 0, :], 0.0)
        tt(pr[:, 1, :], wr[:, :], mag1[:, :], ALU.mult)
        v(tt(pim[:, 1, :], wi[:, :], mag1[:, :], ALU.mult))
        for n in (1, 2, 4):
            b = [z[:, n:n + 1, :].to_broadcast([P, n, GD]) if n > 1 else z[:, 1:2, :] for z in (pr, pim)]
            cmul(pr[:, n + 1:2 * n + 1, :], pim[:, n + 1:2 * n + 1, :], pr[:, 1:n + 1, :], pim[:, 1:n + 1, :],
                 b[0], b[1], n * GD, lambda z: z.rearrange("p (n g) -> p n g", g=GD))
        for src, xp, wp in ((pr, xpr, wpr), (pim, xpi, wpi)):
            cp(xp[:, :, G:GD], src[:, 0:Q, G:GD])
            cp(wp[:, :, 0:G], src[:, 1:Q + 1, 0:G])
            for s in range(Q):
                cp(xp[:, s, 0:G], src[:, Q - 1 - s, 0:G])
                last = cp(wp[:, s, G:GD], src[:, Q - s, G:GD])
        v(last)
        n1, den, gr, gi, t0, t1 = sm[9], sm[12], sm[3], sm[5], sm[6], sm[13]
        ts(n1[:, :], pr[:, 1, :], -1.0, None, ALU.add)
        tt(den[:, :], ar[:, :], ar[:, :], ALU.mult)
        v(tt(t0[:, :], ai[:, :], ai[:, :], ALU.mult))
        v(tt(den[:, :], den[:, :], t0[:, :], ALU.add))
        v(dve.reciprocal(den[:, :], den[:, :]))
        tt(gr[:, :], n1[:, :], ar[:, :], ALU.mult)
        tt(t0[:, :], pim[:, 1, :], ai[:, :], ALU.mult)
        tt(gi[:, :], pim[:, 1, :], ar[:, :], ALU.mult)
        v(tt(t1[:, :], n1[:, :], ai[:, :], ALU.mult))
        tt(gr[:, :], gr[:, :], t0[:, :], ALU.add)
        v(tt(gi[:, :], gi[:, :], t1[:, :], ALU.subtract))
        tt(gr[:, :], gr[:, :], den[:, :], ALU.mult)
        v(tt(gi[:, :], gi[:, :], den[:, :], ALU.mult))
        full = [P, GD, CH]
        grb, gib = (z[:, :].unsqueeze(2).to_broadcast(full) for z in (gr, gi))
        tmp = B[:, 0:GD * CH].rearrange("p (g c) -> p g c", c=CH)
        tt(BA[:, :, :], B1[:, :, :], grb, ALU.mult)
        v(tt(tmp, B2[:, :, :], gib, ALU.mult))
        v(tt(BA[:, :, :], BA[:, :, :], tmp, ALU.add))
        tt(BB[:, :, :], B2[:, :, :], grb, ALU.mult)
        v(tt(tmp, B1[:, :, :], gib, ALU.mult))
        v(tt(BB[:, :, :], BB[:, :, :], tmp, ALU.subtract))

        def matrix(powers_r, powers_i, m1, m2, op):
            for d in range(2):
                g = slice(d * G, (d + 1) * G)
                w = slice(d * G * P, (d + 1) * G * P)
                va, vb = (z.rearrange("p (g s c) -> p s g c", g=G, c=CH) for z in (A[:, w], B[:, w]))
                shape = [P, Q, G, CH]
                br, bi = (z[:, :, g].unsqueeze(3).to_broadcast(shape) for z in (powers_r, powers_i))
                w1_, w2_ = (z[:, g, :].unsqueeze(1).to_broadcast(shape) for z in (m1, m2))
                tt(va, br, w1_, ALU.mult)
                v(tt(vb, bi, w2_, ALU.mult))
                last = tt(A[:, w], A[:, w], B[:, w], op)
            return last
        v(matrix(xpr, xpi, BA, BB, ALU.add))
        for g in range(G):
            last = tt(Dg[:, g, :], dB[:, g * CH:(g + 1) * CH], ident[0:CH, 0:CH], ALU.mult)
        last.then_inc(X_ready, 1)

        for n in range(GD // 4):
            dve.wait_ge(XT_t, n + 1)
            cp(B[:, n * 512:(n + 1) * 512], bank[3 + n % 2][:, :]).then_inc(XT_taken, 1)
        dve.wait_ge(K_ready, 1)
        cp(kF[:, :, :], bank[5][:, 0:G * CH].rearrange("p (g c) -> p g c", c=CH))
        v(cp(kB[:, :, :], bank[6][:, 0:G * CH].rearrange("p (g c) -> p g c", c=CH)))
        v(tt(kB[0:CH], kB[0:CH], Dg[:, :, :], ALU.add))
        tt(kB[0:CH], kB[0:CH], bank[3][0:CH, 0:G * CH].rearrange("p (g c) -> p g c", c=CH), ALU.add).then_inc(K_taken, 1)
        dve.wait_ge(mat_out, 16)
        matrix(wpr, wpi, C1, C2, ALU.add).then_inc(mats, 1)
        dve.wait_ge(mat_out, 32)
        matrix(wpr, wpi, C2, C1, ALU.subtract).then_inc(mats, 1)
        v(cp(k.decay8[:, :], mag8[:, :]))
        for _ in range(3):
            cmul(wr[:, :], wi[:, :], wr[:, :], wi[:, :], wr[:, :], wi[:, :], GD)
        dve.wait_ge(mat_out, 48)
        cosT, sinT = (z[:, 0:GD * SL].rearrange("p (g i) -> p g i", i=SL) for z in (A, B))
        spare = [z[:, GD * SL:GD * (SL + CL // 2)] for z in (A, B)]
        dve.memset(cosT[:, :, 0:1], 1.0)
        v(dve.memset(sinT[:, :, 0:1], 0.0))
        n = 1
        while n <= CL:
            m = min(n, CL + 1 - n)
            shape = [P, GD, m]
            br, bi = (z[:, :].unsqueeze(2).to_broadcast(shape) for z in (wr, wi))
            t0_, t1_ = (x[:, 0:GD * m].rearrange("p (g i) -> p g i", i=m) for x in spare)
            c_lo, s_lo, c_hi, s_hi = cosT[:, :, 0:m], sinT[:, :, 0:m], cosT[:, :, n:n + m], sinT[:, :, n:n + m]
            tt(t0_, c_lo, br, ALU.mult)
            v(tt(t1_, s_lo, bi, ALU.mult))
            tt(c_hi, t0_, t1_, ALU.subtract)
            v(tt(s_hi, c_lo, bi, ALU.mult))
            v(tt(t1_, s_lo, br, ALU.mult))
            v(tt(s_hi, s_hi, t1_, ALU.add))
            if n < CL:
                cmul(wr[:, :], wi[:, :], wr[:, :], wi[:, :], wr[:, :], wi[:, :], GD)
            n *= 2
        cp(cosT[:, :, CL + 1:SL], cosT[:, :, 0:CC + 1])
        cp(sinT[:, :, CL + 1:SL], sinT[:, :, 0:CC + 1]).then_inc(rot_ready, 1)
        rows(4)
        rows(5)

    @block.tensor
    def _(pe):
        n_job = 0
        n_w = 0

        def begin():
            if n_job >= NB:
                pe.wait_ge(acc_taken, n_job - NB + 1)
            return bank[n_job % NB]

        def end(ins):
            nonlocal n_job
            ins.then_inc(acc_ready, 1)
            n_job += 1

        def weights():
            pe.wait_ge(w1_in[n_w % N1], 16 * (n_w // N1 + 1))
            return w1(n_w)

        def done():
            nonlocal n_w
            n_w += 1

        def ada(c):
            w = weights()
            out = begin()
            for kk in range(KD):
                pe.matmul(out[0:33, :], lhsT=cS[:, kk, :], rhs=w[:, kk, :], start=(kk == 0), stop=False)
            end(pe.matmul(out[0:33, :], lhsT=sel[:, c, :], rhs=b12[:, :], start=False, stop=True))
            done()
        pe.wait_ge(k.consts, 1)
        pe.wait_ge(cs_ready, 2)
        pe.wait_ge(small_in, 16)
        ada(0)
        ada(1)
        ada(2)
        pe.wait_ge(s5_in, 16 * NS5)
        for i in range(2):
            pe.transpose(bank[5][:, i * GD:(i + 1) * GD], aa[:, i, :], ident[0:GD, 0:GD])
        pe.transpose(bank[5][:, 2 * GD:3 * GD], h0s[:, :], ident[0:GD, 0:GD]).then_inc(s5_t, 1)
        for i, out in enumerate((bank[6], bank[4])):
            for q in range(4):
                last = pe.transpose(out[:, q * P:(q + 1) * P], cc[i][:, q, :], ident[:, :])
        last.then_inc(c_t, 1)

        def turn(t):
            pe.wait_ge(h_ready, t + 1)
            for h in range(2):
                out = begin()
                for kk in range(4):
                    last = pe.transpose(out[:, kk * P:(kk + 1) * P], xb[t % 2][:, 4 * h + kk:D:KD], ident[:, :])
                end(last)
        for c in range(3, 7):
            ada(c)
        turn(0)
        turn(1)
        ada(7)
        turn(2)
        turn(3)
        w = weights()
        for t in range(NT):
            if t == CTX_T:
                turn(CTX_T)
            pe.wait_ge(acc_taken, at[("xT", (t, 1))] + 1)
            out = begin()
            for kk in range(KD):
                last = pe.matmul(out[:, :], lhsT=hT[:, kk, t * P:(t + 1) * P], rhs=w[:, kk, :],
                                 start=(kk == 0), stop=(kk == KD - 1))
            end(last)
        done()
        def s5_kernels():
            pe.wait_ge(X_ready, 1)
            for n in range(GD // 4):
                if n >= 2:
                    pe.wait_ge(XT_taken, n - 1)
                for g in range(4):
                    last = pe.transpose(bank[3 + n % 2][:, g * P:(g + 1) * P], A[:, (4 * n + g) * P:(4 * n + g + 1) * P],
                                        ident[:, :])
                last.then_inc(XT_t, 1)
            pe.wait_ge(XT_taken, GD // 4)
            for g in range(G):
                col = slice(g * CH, (g + 1) * CH)
                pe.matmul(bank[5][:, col], lhsT=A[:, g * P:(g + 1) * P], rhs=C1[:, g, :], start=True, stop=True)
                b = G + g
                pe.matmul(bank[6][:, col], lhsT=A[:, b * P:(b + 1) * P], rhs=C1[:, b, :], start=True, stop=True)
                last = pe.matmul(bank[3][0:CH, col], lhsT=A[:, g * P + (Q - 1) * CH:(g + 1) * P], rhs=C1[:, g, :],
                                 start=True, stop=True)
            last.then_inc(K_ready, 1)

        for dst in "qk":
            if dst == "k":
                s5_kernels()
            w = weights()
            for j in range(4):
                for lo, n in ((0, LAT), (LAT, CTX)):
                    out = begin()
                    for kk in range(KD):
                        last = pe.matmul(out[:, 0:n], lhsT=w[:, kk, j * P:(j + 1) * P], rhs=hT[:, kk, lo:lo + n],
                                         start=(kk == 0), stop=(kk == KD - 1))
                    end(last)
            done()
        out = begin()
        pe.wait_ge(acc_taken, at[("k", (3, 1))] + 1)
        for j in range(4):
            last = pe.transpose(out[:, j * P:(j + 1) * P], k.kT[:, j, LAT:TOK], ident[:, :])
        end(last)
        w = weights()
        for t in range(NT):
            out = begin()
            for kk in range(KD):
                last = pe.matmul(out[:, :], lhsT=hT[:, kk, t * P:(t + 1) * P], rhs=w[:, kk, :],
                                 start=(kk == 0), stop=(kk == KD - 1))
            end(last)
        done()
        for c in range(8, 12):
            ada(c)
        w = weights()
        for s2 in range(Q // 2):
            out = begin()
            for s in (2 * s2, 2 * s2 + 1):
                for kk in range(KD):
                    last = pe.matmul(out[0:NC, (s % 2) * D_C:(s % 2 + 1) * D_C], lhsT=hT[:, kk, s:TOK:Q],
                                     rhs=w[:, kk, 0:D_C], start=(kk == 0), stop=(kk == KD - 1))
            end(last)
        done()
    scope.close()
    k.clear_sems()


def attend(nc, k, a):
    bank, ident = k.bank, k.ident
    scope = ExitStack()
    sem = k.scoped_sem(scope)
    sb = k.scoped(scope)
    Vw = sb("Vw", [P, 4, 2, D_B])
    cks, cvs = sb("cks", [P, D_B]), sb("cvs", [P, D_B])
    ckT = sb("ckT", [P, 4, P])
    skew = sb("skew", [P, NH, GR * BW])
    maskA = sb("maskA", [P, 3, KC])
    bias = [sb(f"bias{i}", [P, 3, GR, KC]) for i in range(2)]
    prob = [sb(f"prob{i}", [P, KEYS + P]) for i in range(2)]
    pT = [sb(f"pT{i}", [P, KEYS + P]) for i in range(2)]
    wspT = sb("wspT", [P, NH_A, P])
    bsp = sb("bsp", [P, NH_A])
    stats, mv = sb("stats", [P, NT, 6]), sb("mv", [P, NT, 2])
    grms, grstd = sb("grms", [P, NT]), sb("grstd", [P, NT])
    lane_i, cq = sb("lane_i", [P, 1], I32), sb("cq", [P, 1])
    jj, dd, m1, m2 = (sb(n, [P, KC]) for n in ("jj", "dd", "m1", "m2"))
    nmax, psum_, pinv = sb("nmax", [P, 2]), sb("psum_", [P, 2]), sb("pinv", [P, 2])

    cache_in, v_in, skew_in, bsp_in = sem("cache_in"), sem("v_in"), sem("skew_in"), sem("bsp_in")
    iotas, mask_ready = sem("iotas"), sem("mask_ready")
    bias_ready, bias_used = sem("bias_ready"), sem("bias_used")
    var_ready, grms_ready, vn_ready = sem("var_ready"), sem("grms_ready"), sem("vn_ready")
    wsp_t, wsp_taken, gate_ready, ya_ready = sem("wsp_t"), sem("wsp_taken"), sem("gate_ready"), sem("ya_ready")
    ya_t, ya_taken = sem("ya_t"), sem("ya_taken")
    s_ready, max_ready, exp_ready, prob_ready = sem("s_ready"), sem("max_ready"), sem("exp_ready"), sem("prob_ready")
    t_ready, pT_ready, o_ready, o_taken = sem("t_ready"), sem("pT_ready"), sem("o_ready"), sem("o_taken")
    units = [(h, None) for h in range(NH)] + [(h, t) for h in range(NH) for t in range(4)]
    NU = len(units)
    block = scope.enter_context(nc.Block())

    def keys(u):
        return P if units[u][1] is None else KEYS + P

    def query_columns(z, t):
        return z.rearrange("p (r c) -> p r c", c=GW)[:, :, QC * t:QC * (t + 1)]

    @block.sync
    def _(sp):
        sp.dma_start(cks[:, :], a["cache_k"][0, 0].rearrange("l h d -> l (h d)")).then_inc(cache_in, 16)
        sp.dma_start(cvs[:, :], a["cache_v"][0, 0].rearrange("l h d -> l (h d)")).then_inc(cache_in, 16)
        sp.dma_start(bsp[:, :], a["b_sp"][0].rearrange("h i -> i h"), allow_slow_non_contiguous=True).then_inc(bsp_in, 16)
        for r in range(GR):
            sp.dma_start(skew[r * QC:(r + 1) * QC, :, :],
                         k.skewD[:, :, GR - 1 - r:2 * GR - 1 - r, :].rearrange("c h r j -> c h (r j)")).then_inc(skew_in, 16)
        grid = k.vD.rearrange("(r c) d -> r c d", c=GW)
        for t in range(4):
            for half in range(2):
                for r in range(4):
                    sp.dma_start(Vw[r * KC:(r + 1) * KC, t, half, :],
                                 grid[4 * half + r, KC0[t]:KC0[t] + KC, :]).then_inc(v_in, 16)

        for m in range(3):
            sp.dma_start(k.ring[m][:, :], k.matD[m]).then_inc(k.mats_in, 16)
        for s in range(Q):
            sp.dma_start(k.near[s * CH:(s + 1) * CH, :, :].rearrange("p g (t c) -> p g t c", c=CH),
                         k.lagD[:, :, Q - 1 - s:2 * Q - 1 - s, :]).then_inc(k.near_in, 16)
        w_out = a["w_out"][0].rearrange("(k p) n -> p k n", p=P)
        sp.dma_start(k.ring[3][:, :].rearrange("p (k n) -> p k n", k=KD), w_out[:, :, 0:512]).then_inc(k.wout_in[0], 16)

    @block.gpsimd
    def _(pool):
        pool.iota(lane_i[:, :], pattern=[[0, 1]], base=0, channel_multiplier=1).then_inc(iotas, 1)
        pool.iota(jj[:, :], pattern=[[1, KC]], base=0, channel_multiplier=0,
                  allow_small_or_imprecise_dtypes=True).then_inc(iotas, 1)
        pool.wait_ge(mask_ready, 1)
        pool.wait_ge(skew_in, 16 * GR)
        for h in range(NH):
            if h >= 2:
                pool.wait_ge(bias_used, 4 * (h - 1))
            rows = skew[:, h, :].rearrange("p (r j) -> p r j", j=BW)
            for kind, off in enumerate((SHIFT, SHIFT - QC // 2, SHIFT - QC)):
                ins = pool.tensor_tensor(bias[h % 2][:, kind], rows[:, :, off:off + KC],
                                         maskA[:, kind, :].unsqueeze(1).to_broadcast([P, GR, KC]), ALU.add)
            ins.then_inc(bias_ready, 1)

    @block.scalar
    def _(act):
        act.wait_ge(var_ready, 1)
        act.activation(grms[:, :], mv[:, :, 1], ACT.Sqrt, bias=k.eps[:, :]).then_inc(grms_ready, 1)
        act.wait_ge(wsp_t, 1)
        act.activation(wspT[:, :, :], bank[6][:, :].rearrange("p (h n) -> p h n", h=NH_A), ACT.Copy).then_inc(wsp_taken, 1)
        act.activation(ckT[:, :, :], bank[7][:, :].rearrange("p (h n) -> p h n", h=4), ACT.Copy).then_inc(wsp_taken, 1)
        for n in range(3):
            act.wait_ge(ya_t, n + 1)
            if n < 2:
                act.activation(k.mixedT[:, n, 0:LAT], bank[6 + n][:, :], ACT.Copy).then_inc(ya_taken, 1)
            else:
                act.activation(k.mixedT[:, 0:2, LAT:TOK], bank[6][:, 0:2 * P].rearrange("p (c n) -> p c n", c=2),
                               ACT.Copy).then_inc(ya_taken, 1)

        def exps(u):
            act.wait_ge(max_ready, u + 1)
            if u >= 2:
                act.wait_ge(t_ready, u - 1)
            act.activation(prob[u % 2][:, 0:keys(u)], bank[u % 2][:, 0:keys(u)], ACT.Exp, bias=nmax[:, u % 2:u % 2 + 1],
                           accum_out=psum_[:, u % 2:u % 2 + 1]).then_inc(exp_ready, 1)

        def transposed(u):
            act.wait_ge(t_ready, u + 1)
            if u >= 2:
                act.wait_ge(o_ready, u - 1)
            act.activation(pT[u % 2][:, 0:keys(u)], bank[2 + u % 2][:, 0:keys(u)], ACT.Copy).then_inc(pT_ready, 1)
        exps(0)
        for u in range(NU):
            if u + 1 < NU:
                exps(u + 1)
            transposed(u)

    @block.vector
    def _(dve):
        v = k.dve_chain.on(dve)
        tt, ts, stt, cp = dve.tensor_tensor, dve.tensor_scalar, dve.scalar_tensor_tensor, dve.tensor_copy
        gate = slice(D_A, 2 * D_A)
        for t in range(NT):
            last = dve.bn_stats(stats[:, t, :], k.z[:, t, gate])
        v(last)
        for t in range(NT):
            last = dve.bn_aggr(mv[:, t, :], stats[:, t, :])
        last.then_inc(var_ready, 1)
        dve.wait_ge(grms_ready, 1)
        v(dve.reciprocal(grstd[:, :], grms[:, :]))
        for t in range(NT):
            last = ts(k.z[:, t, gate], k.z[:, t, gate], mv[:, t, 0:1], grstd[:, t:t + 1], ALU.subtract, ALU.mult)
        v(last)
        tt(k.z[:, :, gate], k.z[:, :, gate], k.sgu_b[:, :].unsqueeze(1).to_broadcast([P, NT, D_A]),
           ALU.mult).then_inc(vn_ready, 1)
        dve.wait_ge(iotas, 2)
        v(ts(lane_i[:, :], lane_i[:, :], QC - 1, None, ALU.bitwise_and))
        v(cp(cq[:, :], lane_i[:, :]))
        v(ts(dd[:, :], jj[:, :], cq[:, 0:1], None, ALU.subtract))
        half = WIN // 2
        ts(m1[:, :], dd[:, :], float(half), None, ALU.is_lt)
        v(ts(m2[:, :], jj[:, :], float(WIN), None, ALU.is_lt))
        v(tt(m1[:, :], m1[:, :], m2[:, :], ALU.max))
        v(ts(m2[:, :], dd[:, :], float(-half), None, ALU.is_ge))
        v(tt(maskA[:, 0, :], m1[:, :], m2[:, :], ALU.mult))
        ts(m1[:, :], dd[:, :], 0.0, None, ALU.is_ge)
        v(ts(m2[:, :], dd[:, :], float(WIN), None, ALU.is_lt))
        v(tt(maskA[:, 1, :], m1[:, :], m2[:, :], ALU.mult))
        ts(m1[:, :], dd[:, :], float(half), None, ALU.is_ge)
        v(ts(m2[:, :], jj[:, :], float(WIN), None, ALU.is_ge))
        v(tt(m1[:, :], m1[:, :], m2[:, :], ALU.max))
        v(ts(m2[:, :], dd[:, :], float(WIN + half), None, ALU.is_lt))
        v(tt(maskA[:, 2, :], m1[:, :], m2[:, :], ALU.mult))
        ts(maskA[:, :, :], maskA[:, :, :], -NEG, NEG, ALU.mult, ALU.add).then_inc(mask_ready, 1)
        dve.wait_ge(bsp_in, 16)
        for h in range(NH_A):
            dve.wait_ge(gate_ready, h + 1)
            u_h = k.z[:, :, h * HD:(h + 1) * HD]
            stt(u_h, bank[4 + h % 2][:, 0:NT * HD].rearrange("p (t d) -> p t d", d=HD), bsp[:, h:h + 1], u_h,
                ALU.add, ALU.mult).then_inc(ya_ready, 1)

        def top(u):
            h, t = units[u]
            dve.wait_ge(s_ready, u + 1)
            s = bank[u % 2]
            if t is not None:
                dve.wait_ge(bias_ready, h + 1)
                ins = tt(s[:, 0:KEYS], s[:, 0:KEYS], bias[h % 2][:, KIND[t]].rearrange("p r j -> p (r j)"), ALU.add)
                ins.then_inc(bias_used, 1)
                dve.wait_ge(bias_used, 4 * h + t + 1)
            dve.tensor_reduce(nmax[:, u % 2:u % 2 + 1], s[:, 0:keys(u)], axis=AX.X, op=ALU.max,
                              negate=True).then_inc(max_ready, 1)

        def norm(u):
            dve.wait_ge(exp_ready, u + 1)
            v(dve.reciprocal(pinv[:, u % 2:u % 2 + 1], psum_[:, u % 2:u % 2 + 1]))
            ts(prob[u % 2][:, 0:keys(u)], prob[u % 2][:, 0:keys(u)], pinv[:, u % 2:u % 2 + 1], None,
               ALU.mult).then_inc(prob_ready, 1)

        def out(u):
            h, t = units[u]
            dve.wait_ge(o_ready, u + 1)
            lane = slice((h % 2) * HD, (h % 2 + 1) * HD)
            dst = k.mixedT[lane, 2 + h // 2, :]
            dst = dst[:, LAT:TOK] if t is None else query_columns(dst[:, 0:LAT], t)
            src = bank[4 + u % 2][lane, 0:P]
            cp(dst, src if t is None else src.rearrange("p (r c) -> p r c", c=QC)).then_inc(o_taken, 1)
        top(0)
        top(1)
        for u in range(NU):
            norm(u)
            if u + 2 < NU:
                top(u + 2)
            if u >= 2:
                out(u - 2)
        out(NU - 2)
        out(NU - 1)

    @block.tensor
    def _(pe):
        for h in range(NH_A):
            last = pe.transpose(bank[6][:, h * P:(h + 1) * P], k.wsp[:, h, :], ident[:, :])
        pe.wait_ge(cache_in, 32)
        for j in range(4):
            last = pe.transpose(bank[7][:, j * P:(j + 1) * P], cks[:, j * P:(j + 1) * P], ident[:, :])
        last.then_inc(wsp_t, 1)

        def scores(u):
            h, t = units[u]
            if u >= 2:
                pe.wait_ge(exp_ready, u - 1)
            lane = slice((h % 2) * HD, (h % 2 + 1) * HD)
            q, kk = k.qT[lane, h // 2, :], k.kT[lane, h // 2, :]
            out = bank[u % 2]
            if t is None:
                last = pe.matmul(out[:, 0:P], lhsT=q[:, LAT:TOK], rhs=kk[:, LAT:TOK], start=True, stop=True)
            else:
                qt = q[:, t * P:(t + 1) * P]
                kw = kk[:, 0:LAT].rearrange("p (r c) -> p r c", c=GW)[:, :, KC0[t]:KC0[t] + KC]
                pe.matmul(out[:, 0:KEYS], lhsT=qt, rhs=kw, start=True, stop=True)
                last = pe.matmul(out[:, KEYS:KEYS + P], lhsT=qt, rhs=ckT[lane, h // 2, :], start=True, stop=True)
            last.then_inc(s_ready, 1)
        scores(0)
        scores(1)
        pe.wait_ge(wsp_taken, 2)
        pe.wait_ge(vn_ready, 1)
        for h in range(NH_A):
            if h >= 2:
                pe.wait_ge(ya_ready, h - 1)
            pe.matmul(bank[4 + h % 2][:, 0:NT * HD], lhsT=wspT[:, h, :], rhs=k.z[:, :, D_A + h * HD:D_A + (h + 1) * HD],
                      start=True, stop=True).then_inc(gate_ready, 1)
        pe.wait_ge(ya_ready, NH_A)
        for c in range(2):
            for t in range(4):
                last = pe.transpose(bank[6 + c][:, t * P:(t + 1) * P], k.z[:, t, c * P:(c + 1) * P], ident[:, :])
            last.then_inc(ya_t, 1)
        pe.wait_ge(ya_taken, 1)
        for c in range(2):
            last = pe.transpose(bank[6][:, c * P:(c + 1) * P], k.z[:, CTX_T, c * P:(c + 1) * P], ident[:, :])
        last.then_inc(ya_t, 1)

        def turn(u):
            pe.wait_ge(prob_ready, u + 1)
            if u >= 2:
                pe.wait_ge(pT_ready, u - 1)
            for n in range(keys(u) // P):
                last = pe.transpose(bank[2 + u % 2][:, n * P:(n + 1) * P], prob[u % 2][:, n * P:(n + 1) * P], ident[:, :])
            last.then_inc(t_ready, 1)

        def values(u):
            h, t = units[u]
            pe.wait_ge(pT_ready, u + 1)
            if u >= 2:
                pe.wait_ge(o_taken, u - 1)
            pair = slice((h // 2) * P, (h // 2 + 1) * P)
            vals = [k.vctx[:, pair]] if t is None else [Vw[:, t, 0, pair], Vw[:, t, 1, pair], cvs[:, pair]]
            if t == 0 and h == 0:
                pe.wait_ge(v_in, 16 * 32)
            for n, val in enumerate(vals):
                last = pe.matmul(bank[4 + u % 2][:, 0:P], lhsT=val, rhs=pT[u % 2][:, n * P:(n + 1) * P],
                                 start=(n == 0), stop=(n == len(vals) - 1))
            last.then_inc(o_ready, 1)
        for u in range(NU):
            if u + 2 < NU:
                scores(u + 2)
            turn(u)
            if u >= 1:
                values(u - 1)
        values(NU - 1)
    scope.close()
    k.clear_sems()


def scan(nc, k, a):
    bank, ident, ring = k.bank, k.ident, k.ring
    scope = ExitStack()
    sem = k.scoped_sem(scope)
    sb = k.scoped(scope)
    XT, Wc, Ws = (ring[i][:, :] for i in range(3))
    near = k.near
    cosT, sinT, decay = sb("cosT", [P, GD, SL]), sb("sinT", [P, GD, SL]), sb("decay", [P, GD, SL])
    Uf, Ub = sb("Uf", [P, G, SL]), sb("Ub", [P, G, SL])
    vin, turned2 = sb("vin", [P, G, SL]), [sb(f"turned{i}", [P, 4, SL]) for i in range(2)]
    H, cH, sH = sb("H", [P, G, SL]), sb("cH", [P, G, SL]), sb("sH", [P, G, SL])
    yb = sb("yb", [P, G * P])
    y2 = sb("y2", [P, Q, D_C])
    yT, sg = k.hT[:, 0:2, :], k.hT[:, 2, :]
    wg = sb("wg", [P, 2, D_C])
    bg = sb("bg", [P, 2])
    fin = sb("fin", [G, 2, P])
    st = sb("st", [G, 2, 2, NS])

    mats_in, near_in = k.mats_in, k.near_in
    rot_in, glu_in = sem("rot_in"), sem("glu_in")
    u_zero, u_t, u_taken = sem("u_zero"), sem("u_t"), sem("u_taken")
    V_ready, V_taken, b_ready, H_ready, cs_ready = sem("V_ready"), sem("V_taken"), sem("b_ready"), sem("H_ready"), sem("cs_ready2")
    yb_ready, yb_taken, y_ready, y_taken = sem("yb_ready"), sem("yb_taken"), sem("y_ready"), sem("y_taken")
    fin_t, st_ready, st_out = sem("fin_t"), sem("st_ready"), sem("st_out")
    yT_t, yT_taken, z_ready, sg_ready, sg_used = sem("yT_t"), sem("yT_taken"), sem("z_ready"), sem("sg_ready"), sem("sg_used")
    block = scope.enter_context(nc.Block())

    @block.sync
    def _(sp):
        sp.dma_start(cosT[:, :, :], k.rotD[0].rearrange("p (g i) -> p g i", i=SL)).then_inc(rot_in, 16)
        sp.dma_start(sinT[:, :, :], k.rotD[1].rearrange("p (g i) -> p g i", i=SL)).then_inc(rot_in, 16)
        sp.dma_start(wg[:, :, :], a["w_glu"][0].rearrange("(i p) n -> p i n", p=P)).then_inc(glu_in, 16)
        sp.dma_start(bg[:, :], a["b_glu"][0].rearrange("(o p) -> p o", p=P), allow_slow_non_contiguous=True).then_inc(glu_in, 16)
        w_out = a["w_out"][0].rearrange("(k p) n -> p k n", p=P)
        sp.wait_ge(V_ready, 8)
        sp.dma_start(ring[0][:, :].rearrange("p (k n) -> p k n", k=KD), w_out[:, :, 512:1024]).then_inc(k.wout_in[1], 16)
        for n, d in enumerate((1, 0)):
            sp.wait_ge(st_ready, n + 1)
            for part, dst in enumerate((k.outs["new_re"], k.outs["new_im"])):
                sp.dma_start(dst[0, 0, d], st[:, d, part, :]).then_inc(st_out, 16)
        sp.wait_ge(st_out, 64)

    @block.gpsimd
    def _(pool):
        pool.memset(Uf[:, :, :], 0.0)
        pool.memset(Ub[:, :, :], 0.0).then_inc(u_zero, 1)

    GB = 6
    halves = [(z, g0, min(GB, G - g0)) for z in range(2) for g0 in range(0, G, GB)]

    @block.scalar
    def _(act):
        act.wait_ge(u_zero, 1)
        for n, (z, g0, m) in enumerate(halves):
            act.wait_ge(u_t, n + 1)
            src = bank[4 + n % 2][:, 0:m * NC].rearrange("p (g c) -> p g c", c=NC)
            dst = (Uf, Ub)[z]
            act.activation(dst[:, g0:g0 + m, 1:CL + 1], src[:, :, 0:CL], ACT.Copy)
            act.activation(dst[:, g0:g0 + m, CL + 2:SL], src[:, :, CL:NC], ACT.Copy).then_inc(u_taken, 1)
        for n in range(4):
            act.wait_ge(yb_ready, n + 1)
            act.activation(yb[0:NR, n * 512:(n + 1) * 512], bank[4 + n % 2][0:NR, :], ACT.Copy).then_inc(yb_taken, 1)
        for n in range(4):
            act.wait_ge(y_ready, n + 1)
            act.activation(y2[0:NR, :, n * 4 * CH:(n + 1) * 4 * CH].rearrange("p t (g c) -> p g t c", g=4),
                           bank[4 + n % 2][0:NR, :].rearrange("p (g t c) -> p g t c", g=4, c=CH),
                           ACT.Gelu_apprx_tanh).then_inc(y_taken, 1)
        for n in range(4):
            act.wait_ge(yT_t, n + 1)
            h, t4 = n // 2, 4 * (n % 2)
            src = bank[n % 2][:, 0:4 * NR].rearrange("p (t r) -> p t r", r=NR)
            dst = yT[:, h, :].rearrange("p (r t) -> p t r", t=Q)[:, t4:t4 + 4, :]
            act.activation(dst[:, :, 0:CL], src[:, :, 0:CL], ACT.Copy)
            act.activation(dst[:, :, CL:NC], src[:, :, CL + 1:NR], ACT.Copy).then_inc(yT_taken, 1)
        act.wait_ge(glu_in, 32)
        for o in range(2):
            act.wait_ge(z_ready, o + 1)
            if o:
                act.wait_ge(sg_used, 1)
            act.activation(sg[:, 0:LAT], bank[4 + 2 * o][:, :], ACT.Sigmoid, bias=bg[:, o:o + 1])
            act.activation(sg[:, LAT:TOK], bank[5 + 2 * o][:, 0:CTX], ACT.Sigmoid, bias=bg[:, o:o + 1]).then_inc(sg_ready, 1)

    @block.vector
    def _(dve):
        v = k.dve_chain.on(dve)
        tt, cp = dve.tensor_tensor, dve.tensor_copy
        v(dve.memset(decay[:, :, :], 0.0))
        for lo, n in ((1, CL), (CL + 2, CC)):
            cp(decay[:, :, lo:lo + n], k.decay8[:, :].unsqueeze(2).to_broadcast([P, GD, n]))
        dve.wait_ge(rot_in, 32)
        for i, d in enumerate((1, 0)):
            for n in range(4):
                dve.wait_ge(V_ready, 4 * i + n + 1)
                gd = slice(d * G + 4 * n, d * G + 4 * n + 4)
                b = 2 * (n % 2)
                V, W = (bank[b + j][:, 0:4 * SL].rearrange("p (g i) -> p g i", i=SL) for j in range(2))
                out = vin[:, 4 * n:4 * n + 4, :]
                tt(out, V, cosT[:, gd, :], ALU.mult)
                turned = turned2[n % 2]
                tt(turned[:, :, :], W, sinT[:, gd, :], ALU.mult).then_inc(V_taken, 1)
                dve.wait_ge(V_taken, 4 * i + n + 1)
                tt(out[0:NS], out[0:NS], turned[0:NS], ALU.add)
                last = tt(out[NS:P], out[NS:P], turned[NS:P], ALU.subtract)
            v(last)
            v(cp(vin[:, :, 0], k.h0[:, d * G:(d + 1) * G]))
            v(dve.tensor_tensor_scan(H[:, :, :].rearrange("p g i -> p (g i)"),
                                     decay[:, d * G:(d + 1) * G, :].rearrange("p g i -> p (g i)"),
                                     vin[:, :, :].rearrange("p g i -> p (g i)"), 0.0, ALU.mult, ALU.add))
            if i:
                dve.wait_ge(yb_ready, 4)
                dve.wait_ge(fin_t, 1)
            tt(cH[:, :, :], H[:, :, :], cosT[:, d * G:(d + 1) * G, :], ALU.mult)
            tt(sH[:, :, :], H[:, :, :], sinT[:, d * G:(d + 1) * G, :], ALU.mult).then_inc(cs_ready, 1)
            dve.wait_ge(fin_t, i + 1)
            v(cp(fin[:, :, :], bank[6][0:G, 0:2 * P].rearrange("p (x n) -> p x n", x=2)))
            tt(st[:, d, 0, :], fin[:, 0, 0:NS], fin[:, 1, NS:P], ALU.subtract)
            tt(st[:, d, 1, :], fin[:, 0, NS:P], fin[:, 1, 0:NS], ALU.add).then_inc(st_ready, 1)
        for o in range(2):
            dve.wait_ge(sg_ready, o + 1)
            tt(k.mixedT[:, 6 + o, :], yT[:, o, :], sg[:, :], ALU.mult).then_inc(sg_used, 1)

    @block.tensor
    def _(pe):
        for n, (z, g0, m) in enumerate(halves):
            if n >= 2:
                pe.wait_ge(u_taken, n - 1)
            for g in range(m):
                chan = k.pc[0:NC, g0 + g, :, :].rearrange("p s c -> p (s c)")
                out = bank[4 + n % 2][:, g * NC:(g + 1) * NC]
                if z == 0:
                    last = pe.transpose(out, chan, ident[0:NC, 0:NC])
                else:
                    last = pe.matmul(out, lhsT=chan, rhs=k.flip80[0:NC, :], start=True, stop=True)
            last.then_inc(u_t, 1)
        pe.wait_ge(u_taken, len(halves))
        pe.wait_ge(mats_in, 48)
        pe.wait_ge(near_in, 16 * Q)
        for i, d in enumerate((1, 0)):
            src = (Uf, Ub)[d]
            for n in range(4):
                if 4 * i + n >= 2:
                    pe.wait_ge(V_taken, 4 * i + n - 1)
                b = 2 * (n % 2)
                for g in range(4):
                    gd, u = d * G + 4 * n + g, src[:, 4 * n + g, :]
                    col = slice(g * SL, (g + 1) * SL)
                    pe.matmul(bank[b][:, col], lhsT=XT[:, gd * P:(gd + 1) * P], rhs=u, start=True, stop=True)
                    pe.matmul(bank[b + 1][0:NS, col], lhsT=XT[:, gd * P + NS:(gd + 1) * P], rhs=u, start=True, stop=True)
                    last = pe.matmul(bank[b + 1][NS:P, col], lhsT=XT[:, gd * P:gd * P + NS], rhs=u, start=True, stop=True)
                last.then_inc(V_ready, 1)
            pe.wait_ge(cs_ready, i + 1)
            for j, z in enumerate((cH, sH)):
                if i and j == 0:
                    pe.wait_ge(st_ready, 1)
                last = pe.transpose(bank[6][0:G, j * P:(j + 1) * P], z[:, :, SL - 1], ident[:, :])
            last.then_inc(fin_t, 1)
            for n in range(4):
                out = bank[4 + n % 2]
                if i == 0:
                    if n >= 2:
                        pe.wait_ge(yb_taken, n - 1)
                else:
                    pe.wait_ge(yb_taken, 4)
                    if n >= 2:
                        pe.wait_ge(y_taken, n - 1)
                    pe.matmul(out[0:NR, :], lhsT=k.flip[0:NR, 0:NR], rhs=yb[0:NR, n * 512:(n + 1) * 512],
                              start=True, stop=False)
                for g in range(4):
                    gg = 4 * n + g
                    gd, o = d * G + gg, out[0:NR, g * P:(g + 1) * P]
                    w = slice(gd * P, (gd + 1) * P)
                    if i == 0:
                        pe.matmul(o, lhsT=cH[:, gg, 0:NR], rhs=Wc[:, w], start=True, stop=False)
                    else:
                        pe.matmul(o, lhsT=Uf[:, gg, 1:SL], rhs=near[:, gg, :], start=False, stop=False)
                        pe.matmul(o, lhsT=cH[:, gg, 0:NR], rhs=Wc[:, w], start=False, stop=False)
                    last = pe.matmul(o, lhsT=sH[:, gg, 0:NR], rhs=Ws[:, w], start=False, stop=(i == 0 or g == 3))
                last.then_inc(yb_ready if i == 0 else y_ready, 1)
        pe.wait_ge(y_taken, 4)
        for n in range(4):
            h, t4 = n // 2, 4 * (n % 2)
            if n >= 2:
                pe.wait_ge(yT_taken, n - 1)
            for t in range(4):
                last = pe.transpose(bank[n % 2][:, t * NR:(t + 1) * NR], y2[0:NR, t4 + t, h * P:(h + 1) * P],
                                    ident[0:NR, 0:NR])
            last.then_inc(yT_t, 1)
        pe.wait_ge(yT_taken, 4)
        pe.wait_ge(glu_in, 32)
        for o in range(2):
            for j, (lo, n) in enumerate(((0, LAT), (LAT, CTX))):
                out = bank[4 + 2 * o + j]
                if o == 1 and j == 0:
                    pe.wait_ge(st_ready, 2)
                for i in range(2):
                    last = pe.matmul(out[:, 0:n], lhsT=wg[:, i, o * P:(o + 1) * P], rhs=yT[:, i, lo:lo + n],
                                     start=(i == 0), stop=(i == 1))
            last.then_inc(z_ready, 1)
    scope.close()
    k.clear_sems()


def route(nc, k, a, scope, block):
    sem, bank, ident, ring, hT = k.sem, k.bank, k.ident, k.ring, k.hT
    sb = k.scoped(scope)
    gate_b, scale_b, shift_b = sb("gate_b", [P, D]), sb("scale2_b", [P, D]), sb("shift2_b", [P, D])
    tmp = sb("tmp", [P, D])
    h2 = [sb(f"h2_{i}", [P, D]) for i in range(2)]
    ss, ssum, rms, rstd = (sb(n, [P, NT, 2]) for n in ("ss2", "ssum2", "rms2", "rstd2"))
    ss2 = sb("ss3", [P, NT])
    wr = sb("w_rt", [P, KD, NE])
    br = sb("b_rt", [P, NE])
    scores, sel, wts = (sb(n, [P, NT, NE]) for n in ("scores", "sel2", "wts"))
    w = NT * NE
    m8 = shift_b[:, 0:w].rearrange("p (n m) -> p n m", m=8)
    cmp1, cmp2 = (scale_b[:, i * w:(i + 1) * w].rearrange("p (t g h) -> p t g h", t=NT, g=NG) for i in range(2))
    where, hit = (gate_b[:, i * w:(i + 1) * w].rearrange("p (b e) -> p b e", e=NE) for i in range(2))
    msel, rep_ = (z[:, 2 * w:3 * w].rearrange("p (t e) -> p t e", e=NE) for z in (scale_b, gate_b))
    grp, low = sb("grp", [P, NT, NG]), sb("low", [P, NG, NG])
    rank = sb("rank", [P, NT, NG])
    gmask = sb("gmask", [P, NT * NG], I32)
    top8 = sb("top8", [P, NT, 8])
    wsum, winv = sb("wsum", [P, NT]), sb("winv", [P, NT])
    selb = sb("selb", [P, NT, NE], BF16)
    tri = sb("tri", [P, P], BF16)
    ones = sb("ones", [P, P], BF16)
    pos = sb("pos", [P, NT, NE])
    cnt, more, start = sb("cnt", [P, NE]), sb("more", [P, NE]), sb("start", [P, NE])
    eval_, bval = (sb(n, [P, BLK, NE]) for n in ("eval", "bval"))
    lane = k.lane
    entry = sb("entry", [P, 4])
    steps, more_all = sb("steps", [P, 16]), sb("more_all", [P, 1])
    hid = [tmp[:, i * F:(i + 1) * F] for i in range(2)]
    sgate = tmp[:, 2 * F:3 * F]
    hidT = sb("hidT", [P, 2, P])

    b_in, ctx_b, wr_in, ws_in, wsd_in, x_in = sem("b_in"), sem("ctx_b"), sem("wr_in"), sem("ws_in"), sem("wsd_in"), sem("x1_in")
    mix_ready, mix_sq, mix_sum, mix_rms, x1_ready, x1_sq, x1_rms = (
        sem(n) for n in ("mix_ready", "mix_sq", "mix_sum", "mix_rms", "x1_ready", "x1_sq", "x1_rms"))
    h2_ready, h2_t, h2_taken, logit_ready = (sem(n) for n in ("h2_ready", "h2_t", "h2_taken", "logit_ready"))
    h2_sent = [sem(f"h2_sent{i}") for i in range(2)]
    score_ready, iotas, selb_ready, pos_ready, entry_ready, table_t = (
        sem(n) for n in ("score_ready", "iotas4", "selb_ready", "pos_ready", "entry_ready", "table_t"))
    gu_ready, silu_ready, hid_ready, hid_t, hidT_ready, dn_ready, dn_taken = (
        sem(n) for n in ("sgu_ready", "ssilu_ready", "shid_ready", "shid_t", "shidT_ready", "sdn_ready", "sdn_taken"))
    acc_sent, table_ready = sem("acc_sent"), sem("table_ready")
    x_src = [a["x_sample"][0][t * P:(t + 1) * P, :] for t in range(4)] + [a["x_prompt"][0]]
    wout = [ring[3][:, :].rearrange("p (k n) -> p k n", k=KD), ring[0][:, :].rearrange("p (k n) -> p k n", k=KD)]

    @block.sync
    def _(sp):
        for tile, g in ((gate_b, 2), (shift_b, 3), (scale_b, 4)):
            sp.dma_start(tile[:, :], k.modD[1, g].partition_broadcast(P)).then_inc(b_in, 16)
        for t in range(NT):
            sp.dma_start(k.x1[:, t, :], x_src[t]).then_inc(x_in, 16)
        sp.dma_start(wr[:, :, :], a["w_router"][0].rearrange("(p k) e -> p k e", k=KD)).then_inc(wr_in, 16)
        sp.dma_start(br[:, :], a["b_router"][0].partition_broadcast(P)).then_inc(wr_in, 16)
        sp.dma_start(ring[2][:, 0:KD * F], a["w_s_gate"][0].rearrange("(p k) f -> p (k f)", k=KD)).then_inc(ws_in, 16)
        sp.dma_start(ring[2][:, KD * F:2 * KD * F], a["w_s_up"][0].rearrange("(p k) f -> p (k f)", k=KD)).then_inc(ws_in, 16)
        sp.dma_start(k.dn[2][:, :], a["w_s_down"][0].rearrange("(p k) n -> p (k n)", k=2)).then_inc(wsd_in, 16)
        load_gu(sp, k, a, 1, 1)
        load_down(sp, k, a, 1, 1)
        sp.wait_ge(mix_ready, NT)
        load_gu(sp, k, a, 0, 0)
        load_down(sp, k, a, 0, 0)
        load_gu(sp, k, a, 3, 3)
        load_down(sp, k, a, 3, 3)

    @block.gpsimd
    def _(pool):
        pl = k.pool_chain.on(pool)
        pl(pool.memset(tri[:, :], 1.0))
        pl(pool.affine_select(out=tri[:, :], in_=tri[:, :], compare_op=ALU.is_gt, fill=0.0,
                              base=0, pattern=[[1, P]], channel_multiplier=-1))
        pool.memset(ones[:, :], 1.0)
        pl(pool.memset(low[:, :, :], 1.0))
        pl(pool.affine_select(out=low[:, :, :], in_=low[:, :, :], compare_op=ALU.is_gt, fill=0.0,
                              base=0, pattern=[[1, NG], [-1, NG]], channel_multiplier=0))

        def iota(out, pattern, base, cm):
            return pool.iota(out, pattern=pattern, base=base, channel_multiplier=cm,
                             allow_small_or_imprecise_dtypes=True)
        iota(lane[:, :], [[0, 1]], 0, 1)
        iota(eval_[:, :, :], [[0, BLK], [1, NE]], 0, 0)
        iota(bval[:, :, :], [[1, BLK], [0, NE]], -BLK, 0)
        iota(steps[:, :], [[4, 16]], 0, 0)
        iota(k.ids[:, :, 0], [[P, NT]], -TOK, 0)
        iota(k.ids[:, :, 1], [[0, NT]], 0, 1)
        pool.memset(k.ids[:, :, 2], 1.0)
        iota(k.slots[:, :], [[1, (BLK + 1) * P]], 0, 0).then_inc(iotas, 1)
        for t in range(NT):
            if t == CTX_T:
                pool.wait_ge(h2_ready, CTX_T)
                for tile, g in ((gate_b, 2), (shift_b, 3), (scale_b, 4)):
                    pool.dma_start(tile[:, :], k.modD[0, g].partition_broadcast(P)).then_inc(ctx_b, 16)
            pool.wait_ge(h2_ready, t + 1)
            pool.dma_start(k.h2D[t * P:(t + 1) * P, :], h2[t % 2][:, :]).then_inc(h2_sent[t % 2], 16)
        for par in range(2):
            pool.wait_ge(h2_sent[par], 16 * ((NT + 1 - par) // 2))

    def shared_out(act, t):
        act.wait_ge(hid_t, t + 1)
        if t:
            act.wait_ge(dn_ready, t)
        act.activation(hidT[:, :, :], bank[2][:, 0:2 * P].rearrange("p (k n) -> p k n", k=2), ACT.Copy).then_inc(hidT_ready, 1)
        act.wait_ge(dn_ready, t + 1)
        for h in range(2):
            act.activation(k.accs[:, t, h * 512:(h + 1) * 512], bank[4 + h][:, :], ACT.Copy).then_inc(dn_taken, 1)
        act.wait_ge(dn_taken, 2 * t + 2)
        act.dma_start(k.accD[t * P:(t + 1) * P, :], k.accs[:, t, :]).then_inc(acc_sent, 16)

    @block.scalar
    def _(act):
        for t in range(NT):
            act.wait_ge(mix_ready, t + 1)
            for h in range(2):
                act.activation(tmp[:, h * 512:(h + 1) * 512], bank[2 * (t % 2) + h][:, :], ACT.Square,
                               accum_out=ss[:, t, h:h + 1]).then_inc(mix_sq, 1)
            act.wait_ge(mix_sum, t + 1)
            act.activation(rms[:, t, 0:1], ssum[:, t, 0:1], ACT.Sqrt, bias=k.eps[:, :], scale=1.0 / D).then_inc(mix_rms, 1)
            act.wait_ge(x1_ready, t + 1)
            act.activation(tmp[:, :], k.x1[:, t, :], ACT.Square, accum_out=ss2[:, t:t + 1]).then_inc(x1_sq, 1)
            act.wait_ge(x1_sq, t + 1)
            act.activation(rms[:, t, 1:2], ss2[:, t:t + 1], ACT.Sqrt, bias=k.eps[:, :], scale=1.0 / D).then_inc(x1_rms, 1)
            act.wait_ge(h2_t, t + 1)
            for h in range(2):
                act.activation(hT[:, 4 * h:4 * h + 4, t * P:(t + 1) * P],
                               bank[4 + h][:, :].rearrange("p (k n) -> p k n", k=4), ACT.Copy).then_inc(h2_taken, 1)
        act.wait_ge(logit_ready, NT)
        act.activation(scores[:, :, :], bank[6][:, 0:NT * NE].rearrange("p (t e) -> p t e", e=NE),
                       ACT.Sigmoid).then_inc(score_ready, 1)
        for t in range(NT):
            act.wait_ge(gu_ready, t + 1)
            if t:
                act.wait_ge(hid_ready, t)
            act.activation(sgate, bank[t % 2][:, 0:F], ACT.Silu).then_inc(silu_ready, 1)
            if t:
                shared_out(act, t - 1)
        shared_out(act, NT - 1)

    @block.vector
    def _(dve):
        v = k.dve_chain.on(dve)
        tt, ts, stt, cp = dve.tensor_tensor, dve.tensor_scalar, dve.scalar_tensor_tensor, dve.tensor_copy
        dve.wait_ge(b_in, 48)
        dve.wait_ge(x_in, 16 * NT)
        for t in range(NT):
            if t == CTX_T:
                dve.wait_ge(ctx_b, 48)
            x = k.x1[:, t, :]
            dve.wait_ge(mix_sq, 2 * t + 2)
            tt(ssum[:, t, 0:1], ss[:, t, 0:1], ss[:, t, 1:2], ALU.add).then_inc(mix_sum, 1)
            dve.wait_ge(mix_rms, t + 1)
            v(dve.reciprocal(rstd[:, t, 0:1], rms[:, t, 0:1]))
            for h in range(2):
                half = slice(h * 512, (h + 1) * 512)
                last = stt(tmp[:, half], bank[2 * (t % 2) + h][:, :], rstd[:, t, 0:1], gate_b[:, half], ALU.mult, ALU.mult)
            v(last)
            tt(x, x, tmp[:, :], ALU.add).then_inc(x1_ready, 1)
            dve.wait_ge(x1_rms, t + 1)
            v(dve.reciprocal(rstd[:, t, 1:2], rms[:, t, 1:2]))
            if t >= 2:
                dve.wait_ge(h2_sent[t % 2], 16 * (t // 2))
                dve.wait_ge(h2_t, t - 1)
            v(stt(h2[t % 2][:, :], x, rstd[:, t, 1:2], scale_b[:, :], ALU.mult, ALU.mult))
            tt(h2[t % 2][:, :], h2[t % 2][:, :], shift_b[:, :], ALU.add).then_inc(h2_ready, 1)

        def hidden(t):
            dve.wait_ge(silu_ready, t + 1)
            if t >= 2:
                dve.wait_ge(hid_t, t - 1)
            tt(hid[t % 2], sgate, bank[t % 2][:, F:2 * F], ALU.mult).then_inc(hid_ready, 1)

        dve.wait_ge(iotas, 1)
        dve.wait_ge(score_ready, 1)
        bcast = [P, NT, NE]
        v(tt(sel[:, :, :], scores[:, :, :], br[:, :].unsqueeze(1).to_broadcast(bcast), ALU.add))
        selg = sel[:, :, :].rearrange("p t (g e) -> p (t g) e", e=NE // NG)
        for n in range(NT * NG):
            last = dve.max(m8[:, n, :], selg[:, n, :])
        v(last)
        hidden(0)
        v(tt(grp[:, :, :].rearrange("p t g -> p (t g)"), m8[:, :, 0], m8[:, :, 1], ALU.add))
        full = [P, NT, NG, NG]
        mine, other = grp[:, :, :].unsqueeze(3).to_broadcast(full), grp[:, :, :].unsqueeze(2).to_broadcast(full)
        tt(cmp1[:, :, :, :], other, mine, ALU.is_gt)
        v(tt(cmp2[:, :, :, :], other, mine, ALU.is_equal))
        v(tt(cmp2[:, :, :, :], cmp2[:, :, :, :], low[:, :, :].unsqueeze(1).to_broadcast(full), ALU.mult))
        v(tt(cmp1[:, :, :, :], cmp1[:, :, :, :], cmp2[:, :, :, :], ALU.add))
        v(dve.tensor_reduce(rank[:, :, :], cmp1[:, :, :, :], axis=AX.X, op=ALU.add))
        ts(gmask[:, :], rank[:, :, :].rearrange("p t g -> p (t g)"), float(TOPG), None, ALU.is_lt)
        v(dve.memset(msel[:, :, :], NEG))
        v(dve.copy_predicated(msel[:, :, :].rearrange("p t (g e) -> p (t g) e", e=NE // NG),
                              gmask[:, :].unsqueeze(2).to_broadcast([P, NT * NG, NE // NG]), selg))
        for t in range(NT):
            last = dve.max(top8[:, t, :], msel[:, t, :])
        v(last)
        for t in range(NT):
            last = dve.match_replace(rep_[:, t, :], top8[:, t, :], msel[:, t, :], TAKEN)
        v(last)
        hidden(1)
        v(tt(sel[:, :, :], rep_[:, :, :], msel[:, :, :], ALU.not_equal))
        cp(selb[:, :, :], sel[:, :, :]).then_inc(selb_ready, 1)
        v(tt(wts[:, :, :], scores[:, :, :], sel[:, :, :], ALU.mult))
        v(dve.tensor_reduce(wsum[:, :], wts[:, :, :], axis=AX.X, op=ALU.add))
        v(dve.reciprocal(winv[:, :], wsum[:, :]))
        v(ts(winv[:, :], winv[:, :], ROUTE_SCALE, None, ALU.mult))
        v(tt(wts[:, :, :], wts[:, :, :], winv[:, :].unsqueeze(2).to_broadcast(bcast), ALU.mult))
        dve.wait_ge(pos_ready, 1)
        count = bank[7][:, NT * NE:(NT + 1) * NE]
        v(cp(pos[:, :, :], bank[7][:, 0:NT * NE].rearrange("p (t e) -> p t e", e=NE)))
        v(cp(cnt[:, :], count))
        v(stt(pos[:, :, :], pos[:, :, :], 1.0, sel[:, :, :], ALU.add, ALU.mult))
        v(ts(k.place[:, :, :].rearrange("p e t -> p t e"), pos[:, :, :], -1.0, None, ALU.add))
        v(ts(more[:, :], cnt[:, :], float(P), None, ALU.is_gt))
        for b in range(2, BLK):
            v(stt(more[:, :], cnt[:, :], float(b * P), more[:, :], ALU.is_gt, ALU.add))
        v(dve.memset(hit[:, 0, :], 1.0))
        v(dve.tensor_tensor_scan(start[:, :], hit[:, 0, :], more[:, :], 0.0, ALU.mult, ALU.add))
        v(cp(entry[:, 2:3], start[:, NE - 1:NE]))
        v(cp(more_all[:, :], start[:, NE - 1:NE]))
        v(tt(start[:, :], start[:, :], eval_[:, 0, :], ALU.add))
        v(ts(k.done[0:1, :], start[0:1, :], 1.0, None, ALU.add))
        v(tt(where[:, 0, :], start[:, :], more[:, :], ALU.subtract))
        for b in range(1, BLK):
            v(ts(hit[:, b, :], more[:, :], float(b), None, ALU.is_lt))
            v(ts(hit[:, b, :], hit[:, b, :], 1000.0, float(b), ALU.mult, ALU.add))
            v(tt(where[:, b, :], hit[:, b, :], where[:, 0, :], ALU.add))
        v(ts(hit[:, :, :], where[:, :, :], lane[:, 0:1], None, ALU.is_equal))
        flat = lambda z: z[:, :, :].rearrange("p b e -> p (b e)")
        for i, val in enumerate((eval_, bval)):
            v(tt(flat(where), flat(hit), flat(val), ALU.mult))
            v(dve.tensor_reduce(entry[:, i:i + 1], flat(where), axis=AX.X, op=ALU.add))
        v(ts(entry[:, 1:2], entry[:, 1:2], float(BLK), None, ALU.add))
        v(ts(steps[:, :], steps[:, :], entry[:, 2:3], None, ALU.is_lt))
        v(dve.tensor_reduce(entry[:, 2:3], steps[:, :], axis=AX.X, op=ALU.add))
        v(cp(entry[:, 3:4], more_all[:, :]))
        v(stt(entry[:, 3:4], entry[:, 2:3], -float(U), entry[:, 3:4], ALU.mult, ALU.add))
        ts(entry[:, 3:4], entry[:, 3:4], float(U), None, ALU.add)
        ts(entry[:, 2:3], entry[:, 2:3], float(NE // U - 2), None, ALU.add).then_inc(entry_ready, 1)
        hidden(2)
        dve.wait_ge(table_t, 1)
        v(cp(k.table[0:1, 0:4, :], bank[3][0:1, 0:4 * P].rearrange("p (i n) -> p i n", i=4)))
        ts(k.table[0:1, 4, :], k.table[0:1, 0, :], U - 1, None, ALU.bitwise_and).then_inc(table_ready, 1)
        for part in range(3):
            v(cp(k.wparts[:, :, :, part], wts[:, :, :]))
            if part < 2:
                v(tt(wts[:, :, :], wts[:, :, :], k.wparts[:, :, :, part], ALU.subtract))
        k.hidden = hidden

    @block.tensor
    def _(pe):
        pe.wait_ge(k.wout_in[0], 16)
        pe.wait_ge(k.wout_in[1], 16)

        def mixed(t):
            if t >= 2:
                pe.wait_ge(x1_ready, t - 1)
            for h in range(2):
                for kk in range(KD):
                    last = pe.matmul(bank[2 * (t % 2) + h][:, :], lhsT=k.mixedT[:, kk, t * P:(t + 1) * P],
                                     rhs=wout[h][:, kk, :], start=(kk == 0), stop=(kk == KD - 1))
            last.then_inc(mix_ready, 1)

        def turn(t):
            pe.wait_ge(h2_ready, t + 1)
            if t:
                pe.wait_ge(h2_taken, 2 * t)
            for kk in range(KD):
                last = pe.transpose(bank[4 + kk // 4][:, (kk % 4) * P:(kk % 4 + 1) * P], h2[t % 2][:, kk:D:KD], ident[:, :])
            last.then_inc(h2_t, 1)

        def logits(t):
            if t == 0:
                pe.wait_ge(wr_in, 32)
            pe.wait_ge(h2_taken, 2 * t + 2)
            for kk in range(KD):
                last = pe.matmul(bank[6][:, t * NE:(t + 1) * NE], lhsT=hT[:, kk, t * P:(t + 1) * P], rhs=wr[:, kk, :],
                                 start=(kk == 0), stop=(kk == KD - 1))
            last.then_inc(logit_ready, 1)
        mixed(0)
        mixed(1)
        for t in range(NT):
            turn(t)
            if t + 2 < NT:
                mixed(t + 2)
            logits(t)
        pe.wait_ge(ws_in, 32)
        pe.wait_ge(wsd_in, 16)
        gu = ring[2][:, :].rearrange("p (x k f) -> p k x f", x=2, k=KD)
        down = k.dn[2][:, :].rearrange("p (k n) -> p k n", k=2)
        pe.wait_ge(x1_ready, NT)

        def up(t):
            if t >= 2:
                pe.wait_ge(hid_ready, t - 1)
            for kk in range(KD):
                last = pe.matmul(bank[t % 2][:, :].rearrange("p (x f) -> p x f", x=2), lhsT=hT[:, kk, t * P:(t + 1) * P],
                                 rhs=gu[:, kk], start=(kk == 0), stop=(kk == KD - 1))
            last.then_inc(gu_ready, 1)

        def rest(t):
            pe.wait_ge(hid_ready, t + 1)
            if t:
                pe.wait_ge(hidT_ready, t)
            for kk in range(2):
                last = pe.transpose(bank[2][:, kk * P:(kk + 1) * P], hid[t % 2][:, kk:F:2], ident[:, :])
            last.then_inc(hid_t, 1)
            pe.wait_ge(hidT_ready, t + 1)
            if t:
                pe.wait_ge(dn_taken, 2 * t)
            for h in range(2):
                for kk in range(2):
                    last = pe.matmul(bank[4 + h][:, :], lhsT=hidT[:, kk, :], rhs=down[:, kk, h * 512:(h + 1) * 512],
                                     start=(kk == 0), stop=(kk == 1))
            last.then_inc(dn_ready, 1)

        def positions():
            pe.wait_ge(selb_ready, 1)
            pe.wait_ge(iotas, 1)
            for t in range(NT + 1):
                out = bank[7][:, t * NE:(t + 1) * NE]
                for j in range(min(t, NT)):
                    last = pe.matmul(out, lhsT=ones[:, :], rhs=selb[:, j, :], start=(j == 0), stop=(j == t - 1 and t == NT))
                if t < NT:
                    last = pe.matmul(out, lhsT=tri[:, :], rhs=selb[:, t, :], start=(t == 0), stop=True)
            last.then_inc(pos_ready, 1)
        up(0)
        for t in range(NT - 2):
            up(t + 1)
            if t == 2:
                pe.wait_ge(entry_ready, 1)
                for i in range(4):
                    last = pe.transpose(bank[3][0:1, i * P:(i + 1) * P], entry[:, i:i + 1], ident[:, :])
                last.then_inc(table_t, 1)
            rest(t)
            if t == 0:
                positions()
        up(NT - 1)
        k.rest = rest
    k.table_ready, k.acc_sent, k.shared_up = table_ready, acc_sent, gu_ready
    k.xg, k.hid_room, k.hidT_room = h2, shift_b[:, w:w + 2 * F], wr[:, :, :].rearrange("p k e -> p (k e)")


def load_gu(sp, k, a, e, u):
    for h, w in enumerate((a["w_e_gate"][0], a["w_e_up"][0])):
        src = w[e].rearrange("(p k) n -> p (k n)", k=KD) if isinstance(e, int) else \
            w[bass.ds(e, 1)].rearrange("o (p k) n -> p (o k n)", k=KD)
        sp.dma_start(k.ring[u][:, h * KD * F:(h + 1) * KD * F], src).then_inc(k.gu_in[u], 16)


def load_down(sp, k, a, e, u):
    w = a["w_e_down"][0]
    src = w[e].rearrange("(p k) n -> p (k n)", k=2) if isinstance(e, int) else \
        w[bass.ds(e, 1)].rearrange("o (p k) n -> p (o k n)", k=2)
    sp.dma_start(k.dn[u][:, :], src).then_inc(k.dn_in[u], 16)


def experts(nc, k, a, scope, block):
    sem, bank, ident, ring = k.sem, k.bank, k.ident, k.ring
    sb = k.scoped(scope)
    hot = [sb(f"hot{i}", [P, NT, P], BF16) for i in range(2)]
    toks = [sb(f"toks{i}", [P, 1], I32) for i in range(2)]
    dest = [sb(f"dest{i}", [P, 1], I32) for i in range(U)]
    gain = [sb(f"gain{i}", [P, 1]) for i in range(U)]
    info = [sb(f"info{i}", [P, NT, 6], BF16) for i in range(2)]
    got = [sb(f"got{i}", [P, 6]) for i in range(2)]
    miss, place = ([sb(f"{n}{i}", [P, 1]) for i in range(2)] for n in ("miss", "row"))
    spare = k.hT[:, :, :].rearrange("p k n -> p (k n)")
    xg = [z[:, :] for z in k.xg]
    k.gates = [spare[:, (3 + i) * D:(4 + i) * D] for i in range(2)]
    xT = [spare[:, i * D:(i + 1) * D] for i in range(2)]
    sgate = [spare[:, (2 * D + i * F):(2 * D + (i + 1) * F)] for i in range(2)]
    hid = [k.hid_room[:, i * F:(i + 1) * F] for i in range(2)]
    hidT = [k.hidT_room[:, i * F:(i + 1) * F].rearrange("p (k n) -> p k n", k=2) for i in range(2)]
    yo = [k.mixed_flat[:, i * D:(i + 1) * D] for i in range(2)]

    hot_ready, ids_ready, got_ready, sums_ready, toks_ready, dest_ready = (
        sem(n) for n in ("hot_ready", "ids_ready", "got_ready", "sums_ready", "toks_ready", "dest_ready"))
    place_ready, waited = sem("place_ready"), sem("waited")
    gathered = [sem(f"gathered{i}") for i in range(2)]
    xg_t, xT_v, xT_a = sem("xg_t"), sem("xT_v"), sem("xT_a")
    gu_ready, silu_ready, hid_ready, hid_t, hidT_ready = (
        sem(n) for n in ("gu_ready", "silu_ready", "hid_ready", "hid_t", "hidT_ready"))
    dn_ready, yo_ready, added = sem("dn_ready"), sem("yo_ready"), sem("added")
    gu_loaded, dn_loaded = sem("gu_loaded"), sem("dn_loaded")
    MAXSTEP = (NBLK + U - 1) // U

    def last_step(eng):
        before = eng.value_load(k.table[0:1, 2, 0:1], min_val=NE // U - 2, max_val=MAXSTEP - 2)
        return before, before + 1, eng.value_load(k.table[0:1, 3, 0:1], min_val=1, max_val=U)

    def tail(eng, blocks, body):
        body(0)
        for u in range(1, U):
            with eng.If(blocks > u):
                body(u)

    def look(eng, field, i, top):
        at = slice(i, i + 1) if isinstance(i, int) else bass.ds(i, 1)
        return eng.value_load(k.table[0:1, field, at], min_val=0, max_val=top)

    def by_parity(it, n):
        return it * (16 * U // 2) + 16 * n

    @block.sync
    def _(sp):
        sp.wait_ge(k.table_ready, 1)
        sp.wait_ge(xg_t, 1)
        load_gu(sp, k, a, 2, 2)
        load_down(sp, k, a, 2, 2)

        def gate_up(it, u):
            e = it * U + u
            done = sp.value_load(k.done[0:1, e - U:e - U + 1] if isinstance(e, int) else k.done[0:1, bass.ds(e - U, 1)],
                                 min_val=1, max_val=NBLK)
            sp.wait_ge(gu_ready, done)
            load_gu(sp, k, a, e if isinstance(e, int) else sp.snap(e), u)
            sp.wait_ge(k.gu_in[(u + U - 1) % U], it * 32 + (32 if u else 0))
            sp.sem_inc(gu_loaded, 1)

        def down(it, u):
            e = it * U + u
            done = sp.value_load(k.done[0:1, e - U:e - U + 1] if isinstance(e, int) else k.done[0:1, bass.ds(e - U, 1)],
                                 min_val=1, max_val=NBLK)
            sp.wait_ge(dn_ready, done)
            load_down(sp, k, a, e if isinstance(e, int) else sp.snap(e), u)
            sp.wait_ge(k.dn_in[(u + U - 1) % U], it * 16 + (16 if u else 0))
            sp.sem_inc(dn_loaded, 1)
        for u in range(U - 1):
            sp.wait_ge(k.gu_in[u], 32)
            sp.sem_inc(gu_loaded, 1)
            sp.wait_ge(k.dn_in[u], 16)
            sp.sem_inc(dn_loaded, 1)
        for u in range(U):
            gate_up(1, u)
            if u:
                down(1, u - 1)
        with sp.Fori(2, NE // U) as it:
            for u in range(U):
                gate_up(it, u)
                if u:
                    down(it, u - 1)
                else:
                    down(it - 1, U - 1)
        down(NE // U - 1, U - 1)
        sp.wait_ge(k.gu_in[U - 1], NE // U * 32)
        sp.sem_inc(gu_loaded, 1)
        sp.wait_ge(k.dn_in[U - 1], NE // U * 16)
        sp.sem_inc(dn_loaded, 1)
        for i, vec in enumerate((1, 0)):
            sp.dma_start(k.gates[i], k.modD[vec, 5].partition_broadcast(P)).then_inc(k.gate_in, 16)

    @block.gpsimd
    def _(pool):
        def gather(i, par, first=False):
            if not first:
                pool.wait_ge(xg_t, i - 1)
                pool.wait_ge(added, i * 16 - 32)
            pool.wait_ge(toks_ready, i + 1)
            pool.sem_inc(waited, 1)
            pool.indirect_dma_start(out=xg[par], out_offset=None, in_=k.h2D,
                                    in_offset=bass.IndirectOffsetOnAxis(ap=toks[par][:, 0:1], axis=0)).then_inc(gathered[par], 16)
        gather(0, 0, True)
        gather(1, 1, True)
        pool.wait_ge(k.table_ready, 1)
        pool.wait_ge(k.acc_sent, 16 * NT)
        pool.dma_start(k.accD[TOK:TOK + P, :], k.accs[:, NT - 1, :]).then_inc(added, 16)
        pool.wait_ge(xg_t, 1)
        gather(2, 0, True)

        def body(it, u, final=False):
            i = it * U + u
            gather(i + 3, (u + 1) % 2)
            if final:
                pool.wait_ge(gathered[(u + 1) % 2], by_parity(it, (u + 1) // 2 + 2))
            pool.wait_ge(yo_ready, i * 2 + 2)
            pool.wait_ge(dest_ready, i + 1)
            pool.sem_inc(waited, 1)
            pool.indirect_dma_start(out=k.accD, out_offset=bass.IndirectOffsetOnAxis(ap=dest[u][:, 0:1], axis=0),
                                    in_=yo[u % 2], in_offset=None, compute_op=ALU.add).then_inc(added, 16)
        _, last, blocks = last_step(pool)
        with pool.Fori(0, last) as it:
            for u in range(U):
                body(it, u)
        tail(pool, blocks, lambda u: body(last, u, True))
        pool.wait_ge(added, last * (16 * U) + blocks * 16 + 16)

    @block.scalar
    def _(act):
        def turned(i, par):
            act.wait_ge(xg_t, i + 1)
            act.activation(xT[par][:, 512:D], bank[3][:, :], ACT.Copy).then_inc(xT_a, 1)
        turned(0, 0)
        turned(1, 1)
        act.wait_ge(k.table_ready, 1)
        act.wait_ge(k.acc_sent, 16 * NT)

        def body(it, u):
            i, par = it * U + u, u % 2
            act.wait_ge(gu_ready, i + 1)
            act.activation(sgate[par], bank[par][:, 0:F], ACT.Silu).then_inc(silu_ready, 1)
            turned(i + 2, par)
            act.wait_ge(dest_ready, i + 1)
            act.wait_ge(dn_ready, i + 1)
            for h in range(2):
                act.activation(yo[par][:, h * 512:(h + 1) * 512], bank[4 + h][:, :], ACT.Copy,
                               scale=gain[u][:, :]).then_inc(yo_ready, 1)
        _, last, blocks = last_step(act)
        with act.Fori(0, last) as it:
            for u in range(U):
                body(it, u)
        tail(act, blocks, lambda u: body(last, u))

    @block.vector
    def _(dve):
        def onehot(i, par, first=False):
            e, b = look(dve, 0, i, NE - 1), look(dve, 1, i, BLK)
            if not first:
                dve.wait_ge(ids_ready, i - 1)
            shape = [P, NT, P]
            slot = k.slots[:, bass.ds(b * P, P)].unsqueeze(1).to_broadcast(shape)
            place_ = k.place[:, bass.ds(e, 1), :].rearrange("p o t -> p (o t)").unsqueeze(2).to_broadcast(shape)
            dve.tensor_copy(info[par][:, :, 3:6], k.wparts[:, :, bass.ds(e, 1), :].rearrange("p t o n -> p t (o n)"))
            dve.tensor_tensor(hot[par][:, :, :], slot, place_, ALU.is_equal).then_inc(hot_ready, 1)

        def tokens(i, par, u, gathers=None):
            dve.wait_ge(ids_ready, i + 1)
            if gathers is not None:
                dve.wait_ge(gathered[par], gathers)
                dve.wait_ge(added, i * 16 - 32)
            g = got[par]
            dve.tensor_copy(g[:, :], bank[6][:, 0:6]).then_inc(got_ready, 1)
            dve.wait_ge(got_ready, i + 1)
            dve.tensor_tensor(g[:, 0:1], g[:, 0:1], g[:, 1:2], ALU.add)
            dve.tensor_reduce(gain[u][:, :], g[:, 3:6], axis=AX.X, op=ALU.add)
            dve.tensor_scalar(miss[par][:, :], g[:, 2:3], -1.0, 1.0, ALU.mult, ALU.add).then_inc(sums_ready, 1)
            dve.wait_ge(sums_ready, i + 1)
            dve.scalar_tensor_tensor(toks[par][:, :], g[:, 2:3], float(TOK), g[:, 0:1], ALU.mult, ALU.add).then_inc(toks_ready, 1)
            dve.scalar_tensor_tensor(place[par][:, :], k.lane[:, :], miss[par][:, :], g[:, 0:1], ALU.mult, ALU.add).then_inc(place_ready, 1)
            dve.wait_ge(place_ready, i + 1)
            dve.tensor_scalar(dest[u][:, :], place[par][:, :], float(TOK), None, ALU.add).then_inc(dest_ready, 1)

        def turned(i, par):
            dve.wait_ge(xg_t, i + 1)
            dve.tensor_copy(xT[par][:, 0:512], bank[2][:, :]).then_inc(xT_v, 1)
        dve.wait_ge(k.table_ready, 1)
        for par in range(2):
            dve.tensor_copy(info[par][:, :, 0:3], k.ids[:, :, :])
            onehot(par, par, True)
        k.hidden(NT - 2)
        tokens(0, 0, 0)
        k.hidden(NT - 1)
        tokens(1, 1, 1)
        onehot(2, 0)
        onehot(3, 1)
        turned(0, 0)
        dve.wait_ge(gathered[0], 16)
        tokens(2, 0, 2)
        turned(1, 1)

        def body(it, u):
            i, par = it * U + u, u % 2
            dve.wait_ge(silu_ready, i + 1)
            dve.tensor_tensor(hid[par], sgate[par], bank[par][:, F:2 * F], ALU.mult).then_inc(hid_ready, 1)
            dve.wait_ge(hid_t, i + 1)
            dve.tensor_copy(hidT[par], bank[7][:, 0:2 * P].rearrange("p (k n) -> p k n", k=2)).then_inc(hidT_ready, 1)
            turned(i + 2, par)
            tokens(i + 3, 1 - par, (u + 3) % U, gathers=by_parity(it, (u + 1) // 2 + 1))
            onehot(i + 4, par)
        _, last, blocks = last_step(dve)
        with dve.Fori(0, last) as it:
            for u in range(U):
                body(it, u)
        tail(dve, blocks, lambda u: body(last, u))

    @block.tensor
    def _(pe):
        def first(i):
            return isinstance(i, int) and i == 0

        def ids(i, par):
            pe.wait_ge(hot_ready, i + 1)
            if not first(i):
                pe.wait_ge(got_ready, i)
            for t in range(NT):
                last = pe.matmul(bank[6][:, 0:6], lhsT=hot[par][:, t, :], rhs=info[par][:, t, :], start=(t == 0), stop=(t == NT - 1))
            last.then_inc(ids_ready, 1)

        def turn(i, par, gathers):
            pe.wait_ge(gathered[par], gathers)
            if not first(i):
                pe.wait_ge(xT_v, i)
                pe.wait_ge(xT_a, i)
            for kk in range(KD):
                last = pe.transpose(bank[2 + kk // 4][:, (kk % 4) * P:(kk % 4 + 1) * P], xg[par][:, kk:D:KD], ident[:, :])
            last.then_inc(xg_t, 1)

        def gate_up(i, par):
            e, slot = look(pe, 0, i, NE - 1), look(pe, 4, i, U - 1)
            gu = k.rings[:, bass.ds(slot, 1), :].rearrange("p o (x k f) -> p k (o x) f", x=2, k=KD)
            pe.wait_ge(gu_loaded, e + 1)
            pe.wait_ge(xT_v, i + 1)
            pe.wait_ge(xT_a, i + 1)
            for kk in range(KD):
                last = pe.matmul(bank[par][:, :].rearrange("p (x f) -> p x f", x=2), lhsT=xT[par][:, kk * P:(kk + 1) * P],
                                 rhs=gu[:, kk], start=(kk == 0), stop=(kk == KD - 1))
            last.then_inc(gu_ready, 1)

        def ahead(it, u):
            gate_up(it * U + u + 1, 1 - u % 2)

        def body(it, u):
            i, par = it * U + u, u % 2
            e, slot = look(pe, 0, i, NE - 1), look(pe, 4, i, U - 1)
            pe.wait_ge(hid_ready, i + 1)
            for kk in range(2):
                last = pe.transpose(bank[7][:, kk * P:(kk + 1) * P], hid[par][:, kk:F:2], ident[:, :])
            last.then_inc(hid_t, 1)
            turn(i + 2, par, by_parity(it, u // 2 + 2))
            ids(i + 3, 1 - par)
            down = k.downs[:, bass.ds(slot, 1), :].rearrange("p o (k n) -> p (o k) n", k=2)
            pe.wait_ge(dn_loaded, e + 1)
            pe.wait_ge(hidT_ready, i + 1)
            for h in range(2):
                for kk in range(2):
                    last = pe.matmul(bank[4 + h][:, :], lhsT=hidT[par][:, kk, :], rhs=down[:, kk, h * 512:(h + 1) * 512],
                                     start=(kk == 0), stop=(kk == 1))
            last.then_inc(dn_ready, 1)
        ids(0, 0)
        k.rest(NT - 2)
        ids(1, 1)
        k.rest(NT - 1)
        turn(0, 0, 16)
        ids(2, 0)
        turn(1, 1, 16)
        gate_up(0, 0)
        pe.wait_ge(k.table_ready, 1)
        _, last, blocks = last_step(pe)
        with pe.Fori(0, last) as it:
            for u in range(U):
                ahead(it, u)
                body(it, u)

        def final(u):
            if u + 1 < U:
                with pe.If(blocks > u + 1):
                    ahead(last, u)
            body(last, u)
        tail(pe, blocks, final)


def combine(nc, k, a):
    scope = ExitStack()
    sb = k.scoped(scope)
    gate = k.gates
    sq = k.ring[3][:, 0:D]
    total, rms, rstd = (sb(n, [P, NT]) for n in ("total", "rms3", "rstd3"))
    gate_in, sums_in, out_sent = k.gate_in, k.sums_in, k.out_sent
    sums_sq, rms_ready, scaled, out_v, out_p = (k.sem(n) for n in ("sums_sq", "rms_ready", "scaled", "out_v", "out_p"))
    block = scope.enter_context(nc.Block())
    dst = [k.outs["y_s"][0][t * P:(t + 1) * P, :] for t in range(4)] + [k.outs["y_p"][0]]

    @block.sync
    def _(sp):
        for t in range(NT):
            sp.dma_start(k.accs[:, t, :], k.accD[t * P:(t + 1) * P, :]).then_inc(sums_in[t], 16)
        for t in range(NT):
            sp.wait_ge(out_p if t % 2 else out_v, t // 2 + 1)
            sp.dma_start(dst[t], k.accs[:, t, :]).then_inc(out_sent, 16)
        sp.wait_ge(out_sent, 16 * NT)

    @block.scalar
    def _(act):
        for t in range(NT):
            act.wait_ge(sums_in[t], 16)
            if t:
                act.wait_ge(sums_sq, t)
            act.activation(sq, k.accs[:, t, :], ACT.Square, accum_out=total[:, t:t + 1]).then_inc(sums_sq, 1)
            act.wait_ge(sums_sq, t + 1)
            act.activation(rms[:, t:t + 1], total[:, t:t + 1], ACT.Sqrt, bias=k.eps[:, :], scale=1.0 / D).then_inc(rms_ready, 1)

    @block.vector
    def _(dve):
        v = k.dve_chain.on(dve)
        dve.wait_ge(gate_in, 32)
        for t in range(NT):
            acc = k.accs[:, t, :]
            dve.wait_ge(sums_in[t], 16)
            dve.wait_ge(rms_ready, t + 1)
            v(dve.reciprocal(rstd[:, t:t + 1], rms[:, t:t + 1]))
            dve.scalar_tensor_tensor(acc, acc, rstd[:, t:t + 1], gate[t == CTX_T], ALU.mult, ALU.mult).then_inc(scaled, 1)
            if t % 2 == 0:
                dve.wait_ge(scaled, t + 1)
                dve.tensor_tensor(acc, acc, k.x1[:, t, :], ALU.add).then_inc(out_v, 1)

    @block.gpsimd
    def _(pool):
        for t in range(1, NT, 2):
            pool.wait_ge(scaled, t + 1)
            pool.tensor_tensor(k.accs[:, t, :], k.accs[:, t, :], k.x1[:, t, :], ALU.add).then_inc(out_p, 1)
    scope.close()


NAMES = ["x_prompt", "x_sample", "cache_k", "cache_v", "state_ssm_re", "state_ssm_im", "c", "c_ctx",
         "g_pre_mix", "g_post_mix", "g_pre_ffn", "g_post_ffn", "w_ada", "b_ada", "w_in", "w_out",
         "sgu_g", "w_sp", "b_sp", "rpb", "ssm_a_re", "ssm_a_im", "ssm_log_dt", "ssm_b_re", "ssm_b_im",
         "ssm_c_re", "ssm_c_im", "ssm_d", "w_glu", "b_glu", "w_router", "b_router",
         "w_e_gate", "w_e_up", "w_e_down", "w_s_gate", "w_s_up", "w_s_down"]
OUTS = [("y_p", (1, CTX, D)), ("y_s", (1, LAT, D)), ("new_k", (1, 1, CTX, NH, HD)), ("new_v", (1, 1, CTX, NH, HD)),
        ("new_re", (1, 1, 2, G, NS)), ("new_im", (1, 1, 2, G, NS))]


def build(nc, ins, outs):
    ctx = ExitStack()
    with ctx:
        def sem(name):
            return ctx.enter_context(nc.semaphore(name))

        def scoped(stack):
            def sb(name, shape, dt=F32):
                return stack.enter_context(nc.sbuf_tensor(name, shape, dt))
            return sb

        def dram(name, shape):
            return nc.dram_tensor(name, shape, F32, kind="Internal").ap()

        k = Shared()
        k.outs = outs
        k.sem, k.scoped = sem, scoped
        local = []

        def scoped_sem(stack):
            def new(name):
                s = stack.enter_context(nc.semaphore(name))
                local.append(s.num)
                return s
            return new

        def clear_sems():
            nums = sorted(local)
            assert nums == list(range(nums[0], nums[-1] + 1))
            with nc.Block() as block:
                @block.sync
                def _(sp):
                    sp.sem_clear(range(nums[0], nums[-1] + 1))
            local.clear()
        k.scoped_sem, k.clear_sems = scoped_sem, clear_sems
        k.bank = [ctx.enter_context(nc.psum_tensor(f"bank{i}", [P, 512], F32)) for i in range(8)]
        k.modD = dram("modD", [2, 6, D])
        k.vD = dram("vD", [LAT, D_B])
        k.lagD = dram("lagD", [CH, G, 2 * Q - 1, CH])
        k.matD = dram("matD", [3, P, GD * P])
        k.rotD = dram("rotD", [2, P, GD * SL])
        k.skewD = dram("skewD", [QC, NH, 15, BW])
        k.h2D = dram("h2D", [TOK, D])
        k.accD = dram("accD", [TOK + P, D])
        k.pool_chain, k.act_chain, k.dve_chain = (Chain(sem(n)) for n in ("pool_chain", "act_chain", "dve_chain"))
        k.consts = sem("consts")
        k.mats_in, k.near_in = sem("mats_in"), sem("near_in")
        k.wout_in = [sem(f"wout_in{i}") for i in range(2)]
        k.gu_in = [sem(f"gu_in{i}") for i in range(U)]
        k.dn_in = [sem(f"dn_in{i}") for i in range(U)]
        soft = ["rpb_in", "skew_out", "grow_in", "mod_b"]
        soft += [f"x_in{t}" for t in range(NT)] + [f"mod_stored{g}" for g in range(6)]
        k.soft = {name: sem(name) for name in soft}
        k.gate_in, k.out_sent = sem("gate_in"), sem("out_sent")
        k.sums_in = [sem(f"sums_in{i}") for i in range(NT)]
        sb = scoped(ctx)
        k.ident, k.flip, k.flip80, k.eps = sb("ident", [P, P]), sb("flip", [P, NR]), sb("flip80", [P, NC]), sb("eps", [P, 1])
        k.h0, k.decay8 = sb("h0", [P, GD]), sb("decay8", [P, GD])
        k.hT = sb("hT", [P, KD, TOK])
        k.near = k.hT[:, :, :].rearrange("p k n -> p (k n)")[:, 3 * TOK:3 * TOK + G * P].rearrange("p (g n) -> p g n", g=G)
        k.rings = sb("rings", [P, U, 2 * KD * F])
        k.ring = [k.rings[:, i, :] for i in range(U)]
        k.mixedT = sb("mixedT", [P, KD, TOK])
        k.mixed_flat = k.mixedT[:, :, :].rearrange("p k n -> p (k n)")
        k.accs = k.mixed_flat.rearrange("p (t n) -> p t n", t=NT)

        early = ExitStack()
        sb = scoped(early)
        k.pc = sb("pc", [P, G, Q, CH])
        mid = ExitStack()
        sb = scoped(mid)
        k.z = sb("z", [P, NT, 2 * D_A])
        k.qT, k.kT = sb("qT", [P, 4, TOK]), sb("kT", [P, 4, TOK])
        k.vctx = sb("vctx", [P, D_B])
        k.sgu_b, k.wsp = sb("sgu_b", [P, D_A]), sb("wsp", [P, NH_A, P])
        a = ins
        project(nc, k, a)
        attend(nc, k, a)
        mid.close()
        scan(nc, k, a)
        early.close()
        sb = scoped(ctx)
        k.x1 = sb("x1", [P, NT, D])
        k.downs = sb("downs", [P, U, 2 * D])
        k.dn = [k.downs[:, i, :] for i in range(U)]
        k.wparts, k.place = sb("wparts", [P, NT, NE, 3], BF16), sb("place", [P, NE, NT])
        k.table = sb("table", [1, 5, P], I32)
        k.done = sb("done", [1, NE], I32)
        k.slots, k.ids = sb("slots", [P, (BLK + 1) * P]), sb("ids", [P, NT, 3], BF16)
        k.lane = sb("lane", [P, 1])
        moe = ExitStack()
        block = moe.enter_context(nc.Block())
        route(nc, k, a, moe, block)
        experts(nc, k, a, moe, block)
        moe.close()
        combine(nc, k, a)


def kernel(**inputs):
    import concourse.bacc as bacc
    from concourse.bass_utils import run_bass_kernel_spmd

    nc = bacc.Bacc("TRN2", target_bir_lowering=False, num_devices=1)
    arrays = {n: np.ascontiguousarray(inputs[n]) for n in NAMES}
    ins = {n: nc.dram_tensor(n, x.shape, mybir.dt.from_np(x.dtype), kind="ExternalInput").ap() for n, x in arrays.items()}
    outs = {n: nc.dram_tensor(n, shape, F32, kind="ExternalOutput").ap() for n, shape in OUTS}
    build(nc, ins, outs)
    result = run_bass_kernel_spmd(nc, [arrays], core_ids=[0]).results[0]
    return tuple(result[n] for n, _ in OUTS)
```
